# Optimizing a Trainium2 kernel written in Bass

```python
import math
import jax, jax.numpy as jnp
from jax import lax
import numpy as np

D_MODEL = 1024
BATCH = 1
SEQ = 256
DEPTH = 2

GRID_W = 64
Q_BLOCK = 128
EPS = 1e-6
MIN_FORGET = 1e-20

A_HEADS = 6
A_KV_HEADS = 2
A_GROUP = A_HEADS // A_KV_HEADS
A_HEAD_DIM = 64
A_AXIS_DIM = A_HEAD_DIM // 2
ROPE_THETA = 10000.0
A_WIDTH = A_HEADS * A_HEAD_DIM
A_KV_WIDTH = A_KV_HEADS * A_HEAD_DIM

B_HEADS = 4
B_HEAD_DIM = 48
B_V_DIM = 2 * B_HEAD_DIM
B_QK_WIDTH = B_HEADS * 2 * B_HEAD_DIM
B_WIDTH = B_HEADS * B_V_DIM

C_HEADS = 4
C_KEY_DIM = 64
C_VAL_DIM = 64
C_KEY_WIDTH = C_HEADS * C_KEY_DIM
C_VAL_WIDTH = C_HEADS * C_VAL_DIM
C_CHUNK = 16

D_MIX = A_WIDTH + B_WIDTH + C_VAL_WIDTH

IN_SPLITS = (A_WIDTH, A_KV_WIDTH, A_KV_WIDTH,
             B_QK_WIDTH, B_QK_WIDTH, B_WIDTH,
             C_KEY_WIDTH, C_KEY_WIDTH, C_KEY_WIDTH, C_VAL_WIDTH, C_VAL_WIDTH)
IN_COLS = A_WIDTH + 2 * A_KV_WIDTH + 2 * B_QK_WIDTH + B_WIDTH + 3 * C_KEY_WIDTH + 2 * C_VAL_WIDTH

D_FF = 2816
CONV_W = 3


def rms_norm(x, gain):
    xf = x.astype(jnp.float32)
    y = xf * lax.rsqrt(jnp.mean(xf * xf, axis=-1, keepdims=True) + EPS)
    return (y * gain.astype(jnp.float32)).astype(x.dtype)

def split_columns(proj):
    parts, start = [], 0
    for w in IN_SPLITS:
        parts.append(proj[..., start:start + w])
        start += w
    return parts

def axial_rope_tables(seq):
    rows = seq // GRID_W
    row = jnp.repeat(jnp.arange(rows), GRID_W)
    col = jnp.tile(jnp.arange(GRID_W), rows)
    inv_freq = ROPE_THETA ** (-jnp.arange(0, A_AXIS_DIM, 2, dtype=jnp.float32) / A_AXIS_DIM)
    ang = jnp.stack([row, col], axis=-1).astype(jnp.float32)[..., None] * inv_freq
    return jnp.cos(ang), jnp.sin(ang)

def apply_axial_rope(x, cos, sin):
    bsz, seq, heads, d = x.shape
    xf = x.astype(jnp.float32).reshape(bsz, seq, heads, 2, A_AXIS_DIM)
    half = A_AXIS_DIM // 2
    x1, x2 = xf[..., :half], xf[..., half:]
    c, s = cos[None, :, None], sin[None, :, None]
    out = jnp.concatenate([x1 * c - x2 * s, x2 * c + x1 * s], axis=-1)
    return out.reshape(bsz, seq, heads, d).astype(x.dtype)

def alibi_slopes(n_heads):
    return jnp.asarray([2.0 ** (-8.0 * (h + 1) / n_heads) for h in range(n_heads)], jnp.float32)

def hgrn_lower_bounds(logits):
    p = jax.nn.softmax(logits.astype(jnp.float32), axis=0)
    return jnp.maximum(jnp.cumsum(p, axis=0) - p[0:1], 0.0)

def gqa_attention(q, k, v):
    bsz, seq, _, d = q.shape
    nb = seq // Q_BLOCK
    qb = q.reshape(bsz, nb, Q_BLOCK, A_KV_HEADS, A_GROUP, d).transpose(1, 0, 2, 3, 4, 5)
    scale = d ** -0.5

    def one(qblk):
        s = jnp.einsum('bqhgd,bkhd->bhgqk', qblk, k).astype(jnp.float32) * scale
        p = jax.nn.softmax(s, axis=-1).astype(v.dtype)
        return jnp.einsum('bhgqk,bkhd->bqhgd', p, v)

    o = lax.map(one, qb)
    return o.transpose(1, 0, 2, 3, 4, 5).reshape(bsz, seq, A_HEADS * d)

def diff_attention(q1, q2, k1, k2, v, lam, slopes):
    bsz, seq, heads, d = q1.shape
    nb = seq // Q_BLOCK
    scale = d ** -0.5
    pos = jnp.arange(seq)
    qpos = pos.reshape(nb, Q_BLOCK)

    def blocks(t):
        return t.reshape(bsz, nb, Q_BLOCK, heads, d).transpose(1, 0, 2, 3, 4)

    def one(args):
        q1b, q2b, qp = args
        dist = jnp.abs(qp[:, None] - pos[None, :]).astype(jnp.float32)
        bias = -slopes[:, None, None] * dist
        s1 = jnp.einsum('bqhd,bkhd->bhqk', q1b, k1).astype(jnp.float32) * scale + bias
        s2 = jnp.einsum('bqhd,bkhd->bhqk', q2b, k2).astype(jnp.float32) * scale + bias
        p = jax.nn.softmax(s1, axis=-1) - lam * jax.nn.softmax(s2, axis=-1)
        return jnp.einsum('bhqk,bkhv->bqhv', p.astype(v.dtype), v)

    o = lax.map(one, (blocks(q1), blocks(q2), qpos))
    return o.transpose(1, 0, 2, 3, 4).reshape(bsz, seq, heads, v.shape[-1])

def gated_linear_scan(q, k, v, log_f):
    q, k, v, log_f = (t.astype(jnp.float32) for t in (q, k, v, log_f))
    bsz, seq, heads, dk = q.shape
    dv = v.shape[-1]
    n = seq // C_CHUNK

    def chunks(t):
        return t.reshape(bsz, n, C_CHUNK, heads, t.shape[-1]).transpose(0, 3, 1, 2, 4)

    q, k, v, log_f = chunks(q), chunks(k), chunks(v), chunks(log_f)
    b = jnp.cumsum(log_f, axis=3)
    b_end = b[:, :, :, -1:, :]
    lower = jnp.tril(jnp.ones((C_CHUNK, C_CHUNK), dtype=bool))[:, :, None]
    diff = b[:, :, :, :, None, :] - b[:, :, :, None, :, :]
    decay = jnp.where(lower, jnp.exp(jnp.where(lower, diff, 0.0)), 0.0)
    intra = jnp.einsum('bhntd,bhnsd,bhntsd->bhnts', q, k, decay)
    o = jnp.einsum('bhnts,bhnsv->bhntv', intra, v)
    kv_chunk = jnp.einsum('bhnsd,bhnsv->nbhdv', k * jnp.exp(b_end - b), v)
    decay_chunk = jnp.exp(b_end[:, :, :, 0, :]).transpose(2, 0, 1, 3)

    def step(state, inp):
        dec, kv = inp
        return dec[..., None] * state + kv, state

    _, states = lax.scan(step, jnp.zeros((bsz, heads, dk, dv), jnp.float32), (decay_chunk, kv_chunk))
    o = o + jnp.einsum('bhntd,nbhdv->bhntv', q * jnp.exp(b), states)
    return o.transpose(0, 2, 3, 1, 4).reshape(bsz, seq, heads, dv)

def depthwise_conv(h, w, b):
    out = lax.conv_general_dilated(h, w[:, None, :].astype(h.dtype), window_strides=(1,), padding='SAME',
                                   dimension_numbers=('NWC', 'WIO', 'NWC'), feature_group_count=h.shape[-1])
    return out + b.astype(h.dtype)

def first_inputs(seed: int = 0) -> dict:
    key = jax.random.key(seed)
    ks = jax.random.split(key, 17)
    f32 = jnp.float32

    def nrm(k, shape, scale):
        return jax.random.normal(k, shape, f32) * scale

    def gain(k, shape):
        return 1.0 + 0.02 * jax.random.normal(k, shape, f32)

    return {
        'x': nrm(ks[0], (BATCH, SEQ, D_MODEL), 1.0),
        'attn_norm': gain(ks[1], (DEPTH, D_MODEL)),
        'w_in': nrm(ks[2], (DEPTH, D_MODEL, IN_COLS), D_MODEL ** -0.5),
        'a_q_norm': gain(ks[3], (DEPTH, A_HEAD_DIM)),
        'a_k_norm': gain(ks[4], (DEPTH, A_HEAD_DIM)),
        'b_q_norm': gain(ks[5], (DEPTH, B_HEAD_DIM)),
        'b_k_norm': gain(ks[6], (DEPTH, B_HEAD_DIM)),
        'b_lambda': nrm(ks[7], (DEPTH, 4, B_HEAD_DIM), 0.1),
        'b_sub_norm': gain(ks[8], (DEPTH, B_WIDTH)),
        'c_lb_logits': nrm(ks[9], (DEPTH, C_KEY_WIDTH), 0.5),
        'c_out_norm': gain(ks[10], (DEPTH, C_VAL_WIDTH)),
        'w_out': nrm(ks[11], (DEPTH, D_MIX, D_MODEL), D_MIX ** -0.5),
        'ffn_norm': gain(ks[12], (DEPTH, D_MODEL)),
        'w_up': nrm(ks[13], (DEPTH, D_MODEL, 2 * D_FF), D_MODEL ** -0.5),
        'conv_w': nrm(ks[14], (DEPTH, CONV_W, D_FF), CONV_W ** -0.5),
        'conv_b': nrm(ks[15], (DEPTH, D_FF), 0.02),
        'w_down': nrm(ks[16], (DEPTH, D_FF, D_MODEL), D_FF ** -0.5),
    }

def first_block(x, attn_norm, w_in, a_q_norm, a_k_norm, b_q_norm, b_k_norm, b_lambda, b_sub_norm,
              c_lb_logits, c_out_norm, w_out, ffn_norm, w_up, conv_w, conv_b, w_down):
    bsz, seq, _ = x.shape
    cos, sin = axial_rope_tables(seq)
    slopes = alibi_slopes(B_HEADS)
    lb_table = hgrn_lower_bounds(c_lb_logits)

    def rev(t):
        return jnp.flip(t, axis=1)

    for l in range(DEPTH):
        h = rms_norm(x, attn_norm[l])
        proj = h @ w_in[l].astype(h.dtype)
        a_q, a_k, a_v, b_q, b_k, b_v, c_q, c_ff, c_fb, c_v, c_g = split_columns(proj)

        aq = apply_axial_rope(rms_norm(a_q.reshape(bsz, seq, A_HEADS, A_HEAD_DIM), a_q_norm[l]), cos, sin)
        ak = apply_axial_rope(rms_norm(a_k.reshape(bsz, seq, A_KV_HEADS, A_HEAD_DIM), a_k_norm[l]), cos, sin)
        av = a_v.reshape(bsz, seq, A_KV_HEADS, A_HEAD_DIM)
        o_a = gqa_attention(aq, ak, av)

        bq = rms_norm(b_q.reshape(bsz, seq, B_HEADS, 2, B_HEAD_DIM), b_q_norm[l])
        bk = rms_norm(b_k.reshape(bsz, seq, B_HEADS, 2, B_HEAD_DIM), b_k_norm[l])
        bv = b_v.reshape(bsz, seq, B_HEADS, B_V_DIM)
        lam_init = 0.8 - 0.6 * math.exp(-0.3 * l)
        lam_p = b_lambda[l].astype(jnp.float32)
        lam = jnp.exp(jnp.sum(lam_p[0] * lam_p[1])) - jnp.exp(jnp.sum(lam_p[2] * lam_p[3])) + lam_init
        o_b = diff_attention(bq[..., 0, :], bq[..., 1, :], bk[..., 0, :], bk[..., 1, :], bv, lam, slopes)
        o_b = (rms_norm(o_b, b_sub_norm[l].reshape(B_HEADS, B_V_DIM)) * (1.0 - lam_init)).reshape(bsz, seq, B_WIDTH)

        lb = lb_table[l]

        def log_forget(z):
            f = lb + (1.0 - lb) * jax.nn.sigmoid(z.astype(jnp.float32))
            return jnp.log(jnp.maximum(f, MIN_FORGET)).reshape(bsz, seq, C_HEADS, C_KEY_DIM)

        cq = jax.nn.silu(c_q).reshape(bsz, seq, C_HEADS, C_KEY_DIM)
        cv = c_v.reshape(bsz, seq, C_HEADS, C_VAL_DIM)
        lf_fwd = log_forget(c_ff)
        lf_bwd = log_forget(c_fb)
        o_fwd = gated_linear_scan(cq, -jnp.expm1(lf_fwd), cv, lf_fwd)
        o_bwd = rev(gated_linear_scan(rev(cq), rev(-jnp.expm1(lf_bwd)), rev(cv), rev(lf_bwd)))
        o_c = rms_norm(o_fwd + o_bwd, c_out_norm[l].reshape(C_HEADS, C_VAL_DIM)).astype(x.dtype)
        o_c = (o_c * jax.nn.silu(c_g).reshape(bsz, seq, C_HEADS, C_VAL_DIM)).reshape(bsz, seq, C_VAL_WIDTH)

        mix = jnp.concatenate([o_a, o_b.astype(x.dtype), o_c], axis=-1)
        x = x + mix @ w_out[l].astype(x.dtype)

        hf = rms_norm(x, ffn_norm[l]) @ w_up[l].astype(x.dtype)
        gate, val = hf[..., :D_FF], hf[..., D_FF:]
        gate = depthwise_conv(gate, conv_w[l], conv_b[l])
        x = x + (jax.nn.gelu(gate, approximate=False) * val) @ w_down[l].astype(x.dtype)
    return x


HEAD_DIM = 64
D_MIX_2 = D_MODEL
D_FF_2 = 2752
NEG_INF = -1e30
BLOCK = 128
CONV_CH = D_MODEL // 2
CONV_WIDTH = 31
SWA_Q_HEADS = (D_MIX_2 - CONV_CH) // HEAD_DIM
SWA_KV_HEADS = 2
SWA_GROUP = SWA_Q_HEADS // SWA_KV_HEADS
SWA_WINDOW = 128
EVEN_IN = 2 * CONV_CH + (SWA_Q_HEADS + 2 * SWA_KV_HEADS) * HEAD_DIM
DIL_HEADS = 8
DIL_PAIRS = ((128, 1), (512, 4), (2048, 16))
POOL_CH = D_MIX_2 - DIL_HEADS * HEAD_DIM
POOL_SIZES = (2, 4, 8, 16)
POOL_GROUP = POOL_CH // len(POOL_SIZES)
ODD_IN = 3 * DIL_HEADS * HEAD_DIM + POOL_CH
N_EVEN = (DEPTH + 1) // 2
N_ODD = DEPTH // 2


def rms_norm_2(x, g):
    xf = x.astype(jnp.float32)
    y = xf * lax.rsqrt(jnp.mean(xf * xf, axis=-1, keepdims=True) + EPS)
    return (y * g.astype(jnp.float32)).astype(x.dtype)

def layer_norm(x, g, b):
    xf = x.astype(jnp.float32)
    mu = jnp.mean(xf, axis=-1, keepdims=True)
    var = jnp.mean(jnp.square(xf - mu), axis=-1, keepdims=True)
    y = (xf - mu) * lax.rsqrt(var + EPS)
    return (y * g.astype(jnp.float32) + b.astype(jnp.float32)).astype(x.dtype)

def swiglu(x, w_gate, w_up, w_down):
    return (jax.nn.silu(x @ w_gate) * (x @ w_up)) @ w_down

def banded_attention(q, k, v, max_dist, sink=None):
    b, L, kvh, grp, dh = q.shape
    n = -(-L // BLOCK)
    pad = n * BLOCK - L
    qb = jnp.pad(q, ((0, 0), (0, pad), (0, 0), (0, 0), (0, 0))).reshape(b, n, BLOCK, kvh, grp, dh)

    def windows(t):
        tb = jnp.pad(t, ((0, 0), (BLOCK, pad), (0, 0), (0, 0))).reshape(b, n + 1, BLOCK, kvh, dh)
        return jnp.concatenate([tb[:, :-1], tb[:, 1:]], axis=2)

    kw, vw = windows(k), windows(v)
    s = jnp.einsum('bnqhgd,bnkhd->bnhgqk', qb, kw).astype(jnp.float32) * (dh ** -0.5)
    qi = np.arange(BLOCK)[:, None]
    kj = np.arange(2 * BLOCK)[None, :]
    blk = np.arange(n)[:, None, None]
    dist = qi + BLOCK - kj
    valid = (dist >= 0) & (dist <= max_dist) & (blk * BLOCK - BLOCK + kj >= 0)
    s = jnp.where(valid[None, :, None, None], s, NEG_INF)
    m = jnp.max(s, axis=-1)
    if sink is not None:
        m = jnp.maximum(m, sink[None, None, :, :, None])
    p = jnp.exp(s - m[..., None])
    l = jnp.sum(p, axis=-1)
    if sink is not None:
        l = l + jnp.exp(sink[None, None, :, :, None] - m)
    o = jnp.einsum('bnhgqk,bnkhd->bnqhgd', p.astype(v.dtype), vw).astype(jnp.float32)
    m = jnp.moveaxis(m, -1, 2)
    l = jnp.moveaxis(l, -1, 2)
    o = o / l[..., None]

    def to_seq(t):
        return t.reshape(b, n * BLOCK, *t.shape[3:])[:, :L]

    return to_seq(o).astype(q.dtype), to_seq(m), to_seq(l)

def even_mixer(h, w_in, w_out, conv_w, conv_b, ln_g, ln_b, q_g, k_g, sinks):
    b, s, _ = h.shape
    proj = h @ w_in
    cuts = [CONV_CH, 2 * CONV_CH, 2 * CONV_CH + SWA_Q_HEADS * HEAD_DIM,
            2 * CONV_CH + (SWA_Q_HEADS + SWA_KV_HEADS) * HEAD_DIM]
    a_val, a_gate, q, k, v = jnp.split(proj, cuts, axis=-1)
    u = a_val * jax.nn.sigmoid(a_gate)
    u = lax.conv_general_dilated(u, conv_w[:, None, :].astype(u.dtype), (1,), ((CONV_WIDTH - 1, 0),),
                                 dimension_numbers=('NWC', 'WIO', 'NWC'),
                                 feature_group_count=CONV_CH) + conv_b
    u = jax.nn.silu(layer_norm(u, ln_g, ln_b))
    q = rms_norm_2(q.reshape(b, s, SWA_KV_HEADS, SWA_GROUP, HEAD_DIM), q_g)
    k = rms_norm_2(k.reshape(b, s, SWA_KV_HEADS, HEAD_DIM), k_g)
    v = v.reshape(b, s, SWA_KV_HEADS, HEAD_DIM)
    o, _, _ = banded_attention(q, k, v, SWA_WINDOW - 1,
                               sinks.reshape(SWA_KV_HEADS, SWA_GROUP).astype(jnp.float32))
    return jnp.concatenate([u, o.reshape(b, s, -1)], axis=-1) @ w_out

def dilated_branch(q, k, v, window, dilation):
    b, s, h, dh = q.shape
    L = s // dilation

    def to_res(t):
        return t.reshape(b, L, dilation, h, dh).transpose(0, 2, 1, 3, 4).reshape(b * dilation, L, h, dh)

    def from_res(t):
        rest = t.shape[2:]
        return t.reshape(b, dilation, L, *rest).swapaxes(1, 2).reshape(b, s, *rest)

    o, m, l = banded_attention(to_res(q)[:, :, :, None], to_res(k), to_res(v), window // dilation)
    return from_res(o[:, :, :, 0]), from_res(m[..., 0]), from_res(l[..., 0])

def multiscale_pool(u, pool_w, pool_scale):
    b, s, _ = u.shape
    uf = u.astype(jnp.float32)
    cs = jnp.pad(jnp.cumsum(uf, axis=1), ((0, 0), (1, 0), (0, 0)))
    outs = []
    for gi, w in enumerate(POOL_SIZES):
        sl = slice(gi * POOL_GROUP, (gi + 1) * POOL_GROUP)
        c = cs[:, :, sl]
        lagged = jnp.pad(c[:, :s + 1 - w], ((0, 0), (w - 1, 0), (0, 0)))
        count = jnp.minimum(jnp.arange(1, s + 1), w).astype(jnp.float32)[:, None]
        pooled = ((c[:, 1:] - lagged) / count - uf[:, :, sl]).astype(u.dtype)
        outs.append(pooled @ pool_w[gi])
    return jnp.concatenate(outs, axis=-1) * pool_scale

def odd_mixer(h, w_in, w_out, q_g, k_g, pool_w, pool_scale):
    b, s, _ = h.shape
    hd = DIL_HEADS * HEAD_DIM
    q, k, v, u = jnp.split(h @ w_in, [hd, 2 * hd, 3 * hd], axis=-1)
    q = rms_norm_2(q.reshape(b, s, DIL_HEADS, HEAD_DIM), q_g)
    k = rms_norm_2(k.reshape(b, s, DIL_HEADS, HEAD_DIM), k_g)
    v = v.reshape(b, s, DIL_HEADS, HEAD_DIM)
    outs, ms, ls = zip(*[dilated_branch(q, k, v, w, d) for w, d in DIL_PAIRS])
    ms = jnp.stack(ms)
    wts = jnp.stack(ls) * jnp.exp(ms - jnp.max(ms, axis=0))
    att = jnp.einsum('rbsh,rbshd->bshd', wts, jnp.stack(outs).astype(jnp.float32))
    att = (att / jnp.sum(wts, axis=0)[..., None]).astype(h.dtype)
    pool = multiscale_pool(u, pool_w, pool_scale)
    return jnp.concatenate([att.reshape(b, s, hd), pool], axis=-1) @ w_out

def second_inputs(seed: int = 0) -> dict:
    key = jax.random.key(seed)
    ks = jax.random.split(key, 24)

    def nrm(k, shape, scale):
        return scale * jax.random.normal(k, shape, jnp.float32)

    return {
        "x": nrm(ks[0], (BATCH, SEQ, D_MODEL), 1.0),
        "norm_g": 1.0 + nrm(ks[1], (DEPTH, 3, D_MODEL), 0.05),
        "ffn_w_gate": nrm(ks[2], (DEPTH, 2, D_MODEL, D_FF_2), D_MODEL ** -0.5),
        "ffn_w_up": nrm(ks[3], (DEPTH, 2, D_MODEL, D_FF_2), D_MODEL ** -0.5),
        "ffn_w_down": nrm(ks[4], (DEPTH, 2, D_FF_2, D_MODEL), D_FF_2 ** -0.5),
        "ev_w_in": nrm(ks[5], (N_EVEN, D_MODEL, EVEN_IN), D_MODEL ** -0.5),
        "ev_w_out": nrm(ks[6], (N_EVEN, D_MIX_2, D_MODEL), D_MIX_2 ** -0.5),
        "ev_conv_w": nrm(ks[7], (N_EVEN, CONV_WIDTH, CONV_CH), CONV_WIDTH ** -0.5),
        "ev_conv_b": nrm(ks[8], (N_EVEN, CONV_CH), 0.02),
        "ev_ln_g": 1.0 + nrm(ks[9], (N_EVEN, CONV_CH), 0.05),
        "ev_ln_b": nrm(ks[10], (N_EVEN, CONV_CH), 0.02),
        "ev_q_norm_g": 1.0 + nrm(ks[11], (N_EVEN, HEAD_DIM), 0.05),
        "ev_k_norm_g": 1.0 + nrm(ks[12], (N_EVEN, HEAD_DIM), 0.05),
        "ev_sinks": nrm(ks[13], (N_EVEN, SWA_Q_HEADS), 0.5),
        "od_w_in": nrm(ks[14], (N_ODD, D_MODEL, ODD_IN), D_MODEL ** -0.5),
        "od_w_out": nrm(ks[15], (N_ODD, D_MIX_2, D_MODEL), D_MIX_2 ** -0.5),
        "od_q_norm_g": 1.0 + nrm(ks[16], (N_ODD, HEAD_DIM), 0.05),
        "od_k_norm_g": 1.0 + nrm(ks[17], (N_ODD, HEAD_DIM), 0.05),
        "od_pool_w": nrm(ks[18], (N_ODD, len(POOL_SIZES), POOL_GROUP, POOL_GROUP), POOL_GROUP ** -0.5),
        "od_pool_scale": 1.0 + nrm(ks[19], (N_ODD, POOL_CH), 0.05),
    }

def second_block(x, norm_g, ffn_w_gate, ffn_w_up, ffn_w_down,
              ev_w_in, ev_w_out, ev_conv_w, ev_conv_b, ev_ln_g, ev_ln_b,
              ev_q_norm_g, ev_k_norm_g, ev_sinks,
              od_w_in, od_w_out, od_q_norm_g, od_k_norm_g, od_pool_w, od_pool_scale):
    for layer in range(DEPTH):
        g = norm_g[layer]
        x = x + 0.5 * swiglu(rms_norm_2(x, g[0]), ffn_w_gate[layer, 0], ffn_w_up[layer, 0], ffn_w_down[layer, 0])
        h = rms_norm_2(x, g[1])
        i = layer // 2
        if layer % 2 == 0:
            mix = even_mixer(h, ev_w_in[i], ev_w_out[i], ev_conv_w[i], ev_conv_b[i], ev_ln_g[i], ev_ln_b[i],
                             ev_q_norm_g[i], ev_k_norm_g[i], ev_sinks[i])
        else:
            mix = odd_mixer(h, od_w_in[i], od_w_out[i], od_q_norm_g[i], od_k_norm_g[i],
                            od_pool_w[i], od_pool_scale[i])
        x = x + mix
        x = x + 0.5 * swiglu(rms_norm_2(x, g[2]), ffn_w_gate[layer, 1], ffn_w_up[layer, 1], ffn_w_down[layer, 1])
    return x


def setup_inputs(seed=0):
    out = dict(first_inputs(seed))
    for name, value in second_inputs(seed + 1).items():
        if name != "x":
            out[name + "_2"] = value
    return out


def reference(
    x, attn_norm, w_in, a_q_norm, a_k_norm, b_q_norm, b_k_norm, b_lambda, b_sub_norm,
    c_lb_logits, c_out_norm, w_out, ffn_norm, w_up, conv_w, conv_b, w_down, norm_g_2,
    ffn_w_gate_2, ffn_w_up_2, ffn_w_down_2, ev_w_in_2, ev_w_out_2, ev_conv_w_2, ev_conv_b_2,
    ev_ln_g_2, ev_ln_b_2, ev_q_norm_g_2, ev_k_norm_g_2, ev_sinks_2, od_w_in_2, od_w_out_2,
    od_q_norm_g_2, od_k_norm_g_2, od_pool_w_2, od_pool_scale_2,
):
    x = first_block(
        x, attn_norm, w_in, a_q_norm, a_k_norm, b_q_norm, b_k_norm, b_lambda, b_sub_norm,
        c_lb_logits, c_out_norm, w_out, ffn_norm, w_up, conv_w, conv_b, w_down,
    )
    return second_block(
        x, norm_g_2, ffn_w_gate_2, ffn_w_up_2, ffn_w_down_2, ev_w_in_2, ev_w_out_2, ev_conv_w_2,
        ev_conv_b_2, ev_ln_g_2, ev_ln_b_2, ev_q_norm_g_2, ev_k_norm_g_2, ev_sinks_2, od_w_in_2,
        od_w_out_2, od_q_norm_g_2, od_k_norm_g_2, od_pool_w_2, od_pool_scale_2,
    )


_drawn_inputs = setup_inputs


def setup_inputs(seed=0):
    import zlib

    import numpy as np

    out = dict(_drawn_inputs(seed))
    spreads = {}
    factors = {'a_q_norm': 8.0,
     'a_k_norm': 8.0,
     'b_q_norm': 4.32,
     'b_k_norm': 4.499,
     'b_sub_norm': 4.035,
     'c_lb_logits': 3.246,
     'c_out_norm': 6.294,
     'conv_b': 3.641,
     'ev_conv_b_2': 4.69,
     'ev_ln_g_2': 3.803,
     'ev_ln_b_2': 22.419,
     'ev_q_norm_g_2': 8.0,
     'ev_k_norm_g_2': 8.0,
     'ev_sinks_2': 200.0,
     'od_q_norm_g_2': 8.0,
     'od_k_norm_g_2': 8.0,
     'od_pool_scale_2': 9.214}
    for name, (base, spread) in spreads.items():
        noise = np.random.default_rng([zlib.crc32(name.encode()), seed]).standard_normal(out[name].shape)
        drawn = base * np.exp(spread * noise) if base else spread * noise
        out[name] = __import__('jax').numpy.asarray(drawn.astype(out[name].dtype))
    for name, factor in factors.items():
        out[name] = (out[name] * factor).astype(out[name].dtype)
    return out
```

```python
import math

import numpy as np

P = 128
D = 1024
SEQ = 256
DC = D // P
FC = 22
KD = FC // 2
RING = 4
EPS = 1e-6

PHASES = [("mix1", 0), ("ffn1", 0), ("mix1", 1), ("ffn1", 1), ("ffn2", 0), ("even", 0),
          ("ffn2", 1), ("ffn2", 2), ("odd", 0), ("ffn2", 3)]
IN_UNITS = {"mix1": 26, "even": 14, "odd": 16}
UNITS = {"mix1": 26 + 8, "even": 14 + 8, "odd": 16 + 8, "ffn1": 2 * FC + 16, "ffn2": 2 * FC + 16}

M1_AQ, M1_AK, M1_BQ, M1_BK, M1_CQ, M1_CF, M1_CB, M1_AV, M1_BV, M1_CV, M1_CG = 0, 3, 4, 8, 12, 14, 16, 18, 19, 22, 24
A_ORDER = [0, 3, 1, 4, 2, 5]

PRM = {}


def _prm_layout():
    at = 0
    for name, n in [("n1", 2 * 8), ("nf", 2 * 8), ("n2", 6 * 8), ("cw", 2 * 3 * FC), ("cb", 2 * FC), ("aq", 2), ("ak", 2),
                    ("bq", 2), ("bk", 2), ("lb", 4), ("ecw", 31 * 4), ("ecb", 4), ("lng", 4), ("lnb", 4),
                    ("eq", 1), ("ek", 1), ("oq", 1), ("ok", 1), ("ps", 4)]:
        PRM[name] = at
        at += n
    return at


NPRM = _prm_layout()
ROW_LAM, ROW_SUB, ROW_CON, ROW_SINK, NROW = 0, 384, 384 + 768, 384 + 768 + 512, 384 + 768 + 512 + 8
C_ID, C_PERM, C_ONE, C_BLK, C_COS, C_SIN, C_ALI, C_EB, C_OB, C_OC, C_INV = (
    0, 128, 256, 384, 512, 768, 1024, 1024 + 2048, 1024 + 2560, 1024 + 3072, 1024 + 3584)
NCONST = C_INV + 4 * SEQ
LEVELS = [1, 2, 4, 8, 16, 32, 64]


def shape_constants():
    c = np.zeros((P, NCONST), np.float32)
    p = np.arange(P)
    c[:, C_ID:C_ID + P] = np.eye(P)
    c[p, C_PERM + (p ^ 16)] = 1.0
    c[:, C_ONE:C_ONE + P] = 1.0
    c[:, C_BLK:C_BLK + P] = (p[:, None] // 64) == (p[None, :] // 64)
    t = np.arange(SEQ)
    row, col = t // 64, t % 64
    half = 16
    inv = (np.float32(10000.0) ** (-np.arange(0, 32, 2, dtype=np.float32) / np.float32(32))).astype(np.float32)
    axis = (p % 64) // 32
    pos = np.where(axis[:, None] == 0, row[None, :], col[None, :]).astype(np.float32)
    ang = (pos * inv[p % half][:, None]).astype(np.float32)
    c[:, C_COS:C_COS + SEQ] = np.cos(ang)
    c[:, C_SIN:C_SIN + SEQ] = np.sin(ang) * np.where((p % 32) < half, -1.0, 1.0)[:, None]
    q = (np.arange(2)[None, :, None] * P + p[:, None, None])
    k = t[None, None, :]
    d = (q - k)
    for h in range(4):
        c[:, C_ALI + 512 * h:C_ALI + 512 * (h + 1)] = (-(2.0 ** (-2.0 * (h + 1))) * np.abs(d)).reshape(P, 512)
    c[:, C_EB:C_EB + 512] = np.where((d >= 0) & (d <= 127), 0.0, -1e30).reshape(P, 512)
    count = ((d >= 0) & (d <= 128)).astype(int) + ((d >= 0) & (d % 4 == 0)) + ((d >= 0) & (d % 16 == 0))
    c[:, C_OB:C_OB + 512] = np.where(count > 0, 0.0, -1e30).reshape(P, 512)
    c[:, C_OC:C_OC + 512] = count.reshape(P, 512)
    for g, w in enumerate((2, 4, 8, 16)):
        c[:, C_INV + SEQ * g:C_INV + SEQ * (g + 1)] = 1.0 / np.minimum(t + 1, w)
    m = np.zeros((P, len(LEVELS), P), np.float32)
    for n, w in enumerate(LEVELS):
        m[:, n, :] = ((p[:, None] // (2 * w)) == (p[None, :] // (2 * w))) & ((p[:, None] // w) != (p[None, :] // w))
    return c, m.reshape(P, -1)


class Head:

    def __init__(self, rows, d, bias, v, vw, chunk, base, cnt=None, sink=None, h=0):
        self.rows, self.d, self.bias, self.v, self.vw = rows, d, bias, v, vw
        self.chunk, self.base, self.cnt, self.sink, self.h = chunk, base, cnt, sink, h


def build_program(nc, xin, wa, wb, prm_d, row_d, const_d, mask_d, pw_d, out):
    import concourse.bass as bass
    from concourse import mybir
    from contextlib import ExitStack

    f32, r32, u8 = mybir.dt.float32, mybir.dt.float32r, mybir.dt.uint8
    ACT, ALU, AX = mybir.ActivationFunctionType, mybir.AluOpType, mybir.AxisListType
    AP, ds = bass.AP, bass.ds
    NPH = len(PHASES)
    U0 = [sum(UNITS[k] for k, _ in PHASES[:n]) for n in range(NPH + 1)]
    NU = U0[-1]
    is_mix = [k in IN_UNITS for k, _ in PHASES]
    F0 = [FC * sum(not m for m in is_mix[:n]) for n in range(NPH)]
    G0 = [FC * sum(k == "ffn1" for k, _ in PHASES[:n]) for n in range(NPH)]
    Y0 = [sum(IN_UNITS.get(k, 0) for k, _ in PHASES[:n]) for n in range(NPH)]

    def k_tiles(i):
        n = max(n for n in range(NPH) if U0[n] <= i)
        return KD if not is_mix[n] and i - U0[n] >= 2 * FC else DC

    ctx = ExitStack()
    with ctx:
        def sb(name, shape, dt=f32, c=ctx):
            return c.enter_context(nc.sbuf_tensor(name, shape, dt))

        def sem(name):
            return ctx.enter_context(nc.semaphore(name))

        raw = sb("raw", [P, RING, KD * P])
        wh = sb("wh", [P, RING, KD * P], r32)
        wl = sb("wl", [P, RING, KD * P], r32)
        x = sb("x", [P, DC * SEQ])
        hh = sb("hh", [P, DC, SEQ], r32)
        hl = sb("hl", [P, DC, SEQ], r32)
        prm = sb("prm", [P, NPRM])
        row = sb("row", [P, NROW])
        con = sb("con", [P, NCONST])
        msk = sb("msk", [P, len(LEVELS), P], u8)
        poolw = sb("poolw", [P, 4, P])
        sq = sb("sq", [P, 2 * SEQ])
        acc = sb("acc", [P, SEQ])
        sd = sb("sd", [P, SEQ])
        tap = sb("tap", [P, 2, SEQ])
        gu = sb("gu", [P, 2, SEQ])
        eps = sb("eps", [P, 1])
        par = sb("par", [P, 32])
        small = sb("small", [P, 96])
        with ExitStack() as turn:
            guh = sb("guh", [P, FC * SEQ], r32, turn)
            gul = sb("gul", [P, FC * SEQ], r32, turn)
        y = sb("y", [P, 26 * SEQ])
        tv = sb("tv", [P, 2, 1024])
        pr = sb("pr", [P, 4, 2 * SEQ])
        st = sb("st", [P, 2, 2 * SEQ])
        ptb = sb("ptb", [P, 2, 2 * SEQ])
        qq = sb("qq", [P, 2, 2, SEQ])
        kk = sb("kk", [P, 2, 2, SEQ])
        kc = (tap, gu)
        tt = [sb("tt0", [P, 6, SEQ]), sb("tt1", [P, 6, SEQ // 2])]
        at = sb("at", [P, 2, 4, SEQ])

        gb = [ctx.enter_context(nc.psum_tensor(f"gb{n}", [P, 512], f32)) for n in range(4)]
        mb = [ctx.enter_context(nc.psum_tensor(f"mb{n}", [P, 512], f32)) for n in range(4)]

        hf = y[:, 0:DC * SEQ]
        atf = at[:, :, :, :].rearrange("p a b c -> p (a b c)")
        prf = pr[:, :, :].rearrange("p a b -> p (a b)")
        qqf = qq[:, :, :, :].rearrange("p a b c -> p (a b c)")
        kkf = kk[:, :, :, :].rearrange("p a b c -> p (a b c)")
        tmo = y[:, 18 * SEQ:23 * SEQ].rearrange("p (a b) -> p a b", a=2)
        tms = y[:, 12 * SEQ:17 * SEQ].rearrange("p (a b) -> p a b", a=2)
        sgt = y[:, 23 * SEQ:25 * SEQ].rearrange("p (a b) -> p a b", a=2)
        ident = con[:, C_ID:C_ID + P]
        ones = con[:, C_ONE:C_ONE + P]

        def yc(c, n=1):
            return y[:, c * SEQ:(c + n) * SEQ]

        def pair(ap):
            return ap.rearrange("p (a b) -> p a b", a=2)

        def col(name, n=0):
            return prm[:, PRM[name] + n:PRM[name] + n + 1]

        def view(ap, dims):
            return AP(ap.tensor, ap.offset, [list(ap.ap[0])] + dims)

        def level_bank(bank):
            return bank[:, :].rearrange("p (a b c) -> p a b c", a=2, b=2)

        def square_blocks(b):
            return view(at[:, 0, b, 0:1], [[2 * SEQ, 2], [4 * SEQ + P, 2], [1, P]])

        def cross_blocks(b):
            return view(at[:, 0, b, P:P + 1], [[2 * SEQ, 2], [4 * SEQ - P, 2], [1, P]])

        s_raw = [sem(f"raw_loaded{n}") for n in range(RING)]
        s_x0, s_prm, s_con, s_out = sem("x_loaded"), sem("params_loaded"), sem("consts_loaded"), sem("out_written")
        s_hi, s_lo, s_pe = sem("w_hi_ready"), sem("w_lo_ready"), sem("unit_multiplied")
        s_y, s_xo = sem("chunk_projected"), sem("x_updated")
        s_tap, s_c1, s_conv, s_gelu = sem("tap_ready"), sem("second_tap"), sem("conv_ready"), sem("gelu_ready")
        s_gu, s_guh, s_gul = sem("hidden_ready"), sem("hidden_hi_ready"), sem("hidden_lo_ready")
        s_acc, s_ss, s_sd = sem("squares_summed"), sem("x_sum_ready"), sem("x_sd_ready")
        s_hf, s_hh, s_hl = sem("h_ready"), sem("h_hi_ready"), sem("h_lo_ready")
        s_dch, s_pch = sem("vector_step"), sem("gpsimd_step")
        s_eps, s_ini, s_inie = sem("eps_set"), sem("start_values"), sem("start_exps")

        NAMES = ("qk_squared qk_sums qk_sd qk_normed rotated roped v_transposed v_tokens scores maxima exps "
                 "probs probs_turned probsT attn_out attn_copied mix_psum mix_sbuf mix_hi mix_lo").split()
        OWN = {"mix1": ("gate_sigs gates_ready k_packed level_scores diag_copied level_copied totals q_up k_up stats "
                        "stats_sd sigmoids").split(),
               "even": "sigmoids ln_operand ln_sum ln_sd ln_out ln_sig".split(), "odd": ["pooled"]}
        M = {n: {w: sem(f"{k}{l}_{w}") for w in NAMES + OWN[k]}
             for n, (k, l) in enumerate(PHASES) if k in IN_UNITS}

        def norm_gain(n):
            kind, l = PHASES[n]
            return {"mix1": ("n1", 8 * l), "ffn1": ("nf", 8 * l), "even": ("n2", 8), "odd": ("n2", 32),
                    "ffn2": ("n2", 8 * (0, 2, 3, 5)[l % 4])}[kind]

        def qk_groups(kind, l):
            if kind == "mix1":
                gains = [("aq", l)] * 3 + [("ak", l)] + [("bq", l)] * 4 + [("bk", l)] * 4
                dims = [64] * 4 + [48] * 8
            elif kind == "even":
                gains, dims = [("eq", 0)] * 4 + [("ek", 0)], [64] * 5
            else:
                gains, dims = [("oq", 0)] * 4 + [("ok", 0)] * 4, [64] * 8
            return [(c, gains[c:c + 2], dims[c]) for c in range(0, len(gains), 2)]

        V_GROUPS = {"mix1": [(18, 2, 0), (20, 2, 256), (22, 2, 512), (24, 2, 768)], "even": [(5, 1, 0)],
                    "odd": [(8, 2, 0), (10, 2, 256)]}

        def heads(kind):
            if kind == "mix1":
                return ([Head([(M1_AQ + h % 3, M1_AK, 64 * (h // 3))], 64, None, 64 * (h // 3), 64, h % 3, 64 * (h // 3))
                         for h in A_ORDER] +
                        [Head([(M1_BQ + h, M1_BK + h, 0), (M1_BQ + h, M1_BK + h, 64)], 48, C_ALI + 512 * h,
                              128 + 96 * h, 96, None, 0, h=h) for h in range(4)])
            if kind == "even":
                return [Head([(c, 4, 64 * g)], 64, C_EB, 64 * g, 64, 4 + c, 64 * g, sink=c + 4 * g)
                        for c in range(4) for g in range(2)]
            return [Head([(h // 2, 4 + h // 2, 64 * (h % 2))], 64, C_OB, 64 * h, 64, h // 2, 64 * (h % 2), cnt=C_OC)
                    for h in range(8)]

        def row0(hs, t):
            return sum(len(h.rows) for h in hs[:t])

        def beside(kind):
            plan = {}
            for g, (c, gains, _) in enumerate(qk_groups(kind, 0)):
                plan.setdefault(c + len(gains) + 2, []).append(("norm", g))
            if kind == "mix1":
                plan.setdefault(8, []).append(("rope", 0))
                plan.setdefault(10, []).append(("rope", 1))
                plan.setdefault(20, []).append(("gates", 0))
            for v, (c, w, _) in enumerate(V_GROUPS[kind]):
                plan.setdefault(c + w + 1, []).append(("turn", v))
            for c in range(4):
                if kind == "even":
                    plan.setdefault(9 + 2 * c, []).append(("conv", c))
                if kind == "odd":
                    plan.setdefault(14 + c, []).append(("pool", c))
            return plan

        NL = len(LEVELS)
        FIRST = {"mix1": 0, "even": 4, "odd": 4}
        MIX_GROUPS = {"mix1": 6, "even": 8, "odd": 8}

        block = ctx.enter_context(nc.Block())

        @block.sync
        def _(sp):
            sp.dma_start(x[:, :], xin).then_inc(s_x0, 16)
            sp.dma_start(prm[:, :], prm_d).then_inc(s_prm, 16)
            na = nb = 0

            def load(i, slot, src, width):
                if not isinstance(i, int) or i >= RING:
                    sp.wait_ge(s_lo, i - (RING - 1))
                sp.dma_start(raw[:, slot, 0:width], src).then_inc(s_raw[slot], 16)

            for n, (kind, l) in enumerate(PHASES):
                if is_mix[n]:
                    for u in range(UNITS[kind]):
                        i = U0[n] + u
                        load(i, i % RING, wa[na + u, :, :], DC * P)
                    na += UNITS[kind]
                else:
                    with sp.Fori(0, FC // 2) as it:
                        for j in range(4):
                            i = U0[n] + j
                            load(it * 4 + i, i % RING, AP(wa.tensor, it * (4 * P * DC * P) + (na + j) * (P * DC * P),
                                                          [[DC * P, P], [1, DC * P]]), DC * P)
                    na += 2 * FC
                    with sp.Fori(0, 4) as it:
                        for j in range(4):
                            i = U0[n] + 2 * FC + j
                            load(it * 4 + i, i % RING, AP(wb.tensor, it * (4 * P * KD * P) + (nb + j) * (P * KD * P),
                                                          [[KD * P, P], [1, KD * P]]), KD * P)
                    nb += 16
            for c in range(DC):
                sp.wait_ge(s_xo, DC * (NPH - 1) + c + 1)
                sp.dma_start(out[:, c * SEQ:(c + 1) * SEQ], x[:, c * SEQ:(c + 1) * SEQ]).then_inc(s_out, 16)
            sp.wait_ge(s_out, 16 * DC)

        @block.gpsimd
        def _(pool):
            steps = [0]

            def link(ins):
                steps[0] += 1
                ins.then_inc(s_pch, 1)
                pool.wait_ge(s_pch, steps[0])

            pool.dma_start(con[:, :], const_d).then_inc(s_con, 16)
            pool.dma_start(row[:, :], AP(row_d.tensor, 0, [[0, P], [1, NROW]])).then_inc(s_con, 16)
            pool.dma_start(prf[:, 0:NL * P], mask_d).then_inc(s_con, 16)
            pool.dma_start(poolw[:, :, :], pw_d).then_inc(s_con, 16)
            nc.gpsimd.memset(eps[:, :], EPS).then_inc(s_eps, 1)

            def norm(n):
                for c in range(DC):
                    if n == 0:
                        pool.wait_ge(s_x0, 16)
                    else:
                        pool.wait_ge(s_xo, DC * (n - 1) + c + 1)
                    xc = x[:, c * SEQ:(c + 1) * SEQ]
                    if c == 0:
                        link(nc.gpsimd.tensor_tensor(acc[:, :], xc, xc, ALU.mult))
                    else:
                        link(nc.gpsimd.tensor_tensor(sq[:, 0:SEQ], xc, xc, ALU.mult))
                        ins = nc.gpsimd.tensor_tensor(acc[:, :], acc[:, :], sq[:, 0:SEQ], ALU.add)
                        if c < DC - 1:
                            link(ins)
                        else:
                            ins.then_inc(s_acc, 1)
                for c in range(DC):
                    pool.wait_ge(s_hh, DC * n + c + 1)
                    nc.gpsimd.tensor_tensor(hl[:, c, :], hf[:, c * SEQ:(c + 1) * SEQ], hh[:, c, :].bitcast(f32),
                                            ALU.subtract).then_inc(s_hl, 1)

            def key_levels(m):
                pool.wait_ge(m["gates_ready"], 1)
                for b, w in enumerate(LEVELS):
                    src, dst, nblk = tt[b % 2], tt[(b + 1) % 2], SEQ // w
                    step = src.shape[-1]
                    pool.wait_ge(m["k_packed"], b + 1)
                    if b == 0:
                        pool.wait_ge(m["level_scores"], 1)
                    if b >= 1:
                        pool.wait_ge(m["totals"], b)
                    for hp in range(2):
                        kv = view(kk[:, hp, 0, 0:1], [[2 * w, nblk // 2], [SEQ + w, 2], [1, w]])
                        tot = view(src[:, 3 * hp + 1, 1:2], [[2, nblk // 2], [step - 1, 2], [0, w]])
                        ins = nc.gpsimd.tensor_tensor(kv, kv, tot, ALU.mult)
                    ins.then_inc(m["k_up"], 1)
                    if b < NL - 1:
                        if b >= 1:
                            pool.wait_ge(m["q_up"], b)
                        pool.wait_ge(m["k_up"], b + 1)
                        nc.gpsimd.tensor_tensor(view(dst[:, 0, 0:1], [[dst.shape[-1], 6], [1, nblk // 2]]),
                                                view(src[:, 0, 0:1], [[step, 6], [2, nblk // 2]]),
                                                view(src[:, 0, 1:2], [[step, 6], [2, nblk // 2]]),
                                                ALU.mult).then_inc(m["totals"], 1)

            for n, (kind, l) in enumerate(PHASES):
                norm(n)
                if is_mix[n]:
                    m = M[n]
                    for g, (c, gains, _) in enumerate(qk_groups(kind, l)):
                        w = len(gains) * SEQ
                        pool.wait_ge(s_y, Y0[n] + c + len(gains))
                        if g >= 1:
                            pool.wait_ge(m["qk_sums"], g)
                        nc.gpsimd.tensor_tensor(sq[:, 0:w], yc(c, len(gains)), yc(c, len(gains)), ALU.mult).then_inc(m["qk_squared"], 1)
                    if kind == "mix1":
                        key_levels(m)
                else:
                    F = F0[n]
                    with pool.Fori(0, FC // 2) as it:
                        for j in range(2):
                            part = ds(it * (2 * SEQ) + j * SEQ, SEQ)
                            pool.wait_ge(s_guh, it * 2 + (F + j + 1))
                            nc.gpsimd.tensor_tensor(gul[:, part], gu[:, j, :], guh[:, part].bitcast(f32),
                                                    ALU.subtract).then_inc(s_gul, 1)

        @block.scalar
        def _(act):
            def split(i, slot, nt, loaded):
                act.wait_ge(s_raw[slot], loaded)
                if not isinstance(i, int) or i >= RING:
                    act.wait_ge(s_pe, i - (RING - 1))
                nc.scalar.activation(wh[:, slot, 0:nt * P], raw[:, slot, 0:nt * P], ACT.Copy).then_inc(s_hi, 1)

            def split_next(i):
                if i < NU:
                    split(i, i % RING, k_tiles(i), 16 * (i // RING + 1))

            def norm(n):
                act.wait_ge(s_ss, n + 1)
                nc.scalar.activation(sd[:, :], mb[0][:, 0:SEQ], ACT.Sqrt, bias=eps[:, 0:1], scale=1.0 / D).then_inc(s_sd, 1)
                for c in range(DC):
                    act.wait_ge(s_hf, DC * n + c + 1)
                    nc.scalar.activation(hh[:, c, :], hf[:, c * SEQ:(c + 1) * SEQ], ACT.Copy).then_inc(s_hh, 1)

            def softmax_exp(m, hs, t):
                h = hs[t]
                if t >= 2:
                    act.wait_ge(m["probs_turned"], t - 1)
                for k in range(len(h.rows)):
                    r = row0(hs, t) + k
                    act.wait_ge(m["maxima"], r + 1)
                    for qt in range(2):
                        cs = slice(qt * SEQ, (qt + 1) * SEQ)
                        o = 2 * (r % 4) + qt
                        src, scale = (mb[r % 2][:, cs], h.d ** -0.5) if h.bias is None else (st[:, r % 2, cs], 1.0)
                        acc_out = None if h.cnt is not None else small[:, 8 + o:9 + o]
                        ins = nc.scalar.activation(pr[:, r % 4, cs], src, ACT.Exp, bias=small[:, o:o + 1], scale=scale,
                                                   accum_out=acc_out)
                    if h.sink is not None:
                        for qt in range(2):
                            o = 2 * (r % 4) + qt
                            ins = nc.scalar.activation(small[:, 24 + o:25 + o], row[:, ROW_SINK + h.sink:ROW_SINK + h.sink + 1],
                                                       ACT.Exp, bias=small[:, o:o + 1])
                    ins.then_inc(m["exps"], 1)

            def pack_keys(m, v):
                w = LEVELS[v - 1]
                if v == 1:
                    act.wait_ge(m["gates_ready"], 1)
                else:
                    act.wait_ge(m["k_up"], v - 1)
                if v >= 3:
                    act.wait_ge(m["level_scores"], v - 1)
                for hp in range(2):
                    ins = nc.scalar.activation(kc[v % 2][:, hp, :].rearrange("p (a b c) -> p a b c", b=2, c=w),
                                               view(kk[:, hp, 0, 0:1], [[2 * w, SEQ // (2 * w)], [SEQ + w, 2], [1, w]]),
                                               ACT.Copy)
                ins.then_inc(m["k_packed"], 1)

            def attention(m, kind):
                hs = heads(kind)
                if kind == "mix1":
                    pack_keys(m, 1)
                for t in range(len(hs) + 3):
                    if t < len(hs):
                        softmax_exp(m, hs, t)
                    if kind == "mix1" and t == 1:
                        act.wait_ge(m["level_scores"], 1)
                        for b in range(2):
                            nc.scalar.activation(square_blocks(b), level_bank(gb[b]), ACT.Copy).then_inc(m["diag_copied"], 1)
                    if kind == "mix1" and t == NL + 2:
                        act.wait_ge(m["level_scores"], NL + 2)
                        for b in range(2):
                            nc.scalar.activation(cross_blocks(b), level_bank(gb[b]), ACT.Copy).then_inc(m["diag_copied"], 1)
                    if kind == "mix1" and 1 <= t < NL:
                        pack_keys(m, t + 1)
                    if 1 <= t <= len(hs):
                        j = t - 1
                        act.wait_ge(m["probs_turned"], j + 1)
                        if j >= 2:
                            act.wait_ge(m["attn_out"], j - 1)
                        nc.scalar.activation(ptb[:, j % 2, :], mb[2][:, :], ACT.Copy).then_inc(m["probsT"], 1)
                    if 2 <= t < len(hs) + 2:
                        j = t - 2
                        h = hs[j]
                        if h.chunk is None:
                            act.wait_ge(m["attn_out"], j + 1)
                            nc.scalar.activation(tmo[:, :, 96 * h.h:96 * (h.h + 1)], pair(mb[3][:, :])[:, :, 0:96],
                                                 ACT.Copy).then_inc(m["attn_copied"], 1)
                        elif j % 2 == 1:
                            act.wait_ge(m["attn_out"], j + 1)
                            half = (j // 2) % 2
                            nc.scalar.activation(hh[:, h.chunk, :], mb[3][:, half * SEQ:(half + 1) * SEQ],
                                                 ACT.Copy).then_inc(m["mix_hi"], 1)

            def mixer(n, kind, l):
                m, nin, plan = M[n], IN_UNITS[kind], beside(kind)
                groups, vg = qk_groups(kind, l), V_GROUPS[kind]
                for u in range(max(nin, max(plan) + 1)):
                    if u < nin:
                        split_next(U0[n] + u + RING)
                        act.wait_ge(s_pe, U0[n] + u + 1)
                        nc.scalar.activation(yc(u), gb[u % 4][:, 0:SEQ], ACT.Copy).then_inc(s_y, 1)
                    for what, g in plan.get(u, []):
                        if what == "norm":
                            w = len(groups[g][1]) * SEQ
                            act.wait_ge(m["qk_sums"], g + 1)
                            if g >= 2:
                                act.wait_ge(m["qk_normed"], g - 1)
                            nc.scalar.activation(st[:, g % 2, 0:w], mb[g % 2][:, 0:w], ACT.Sqrt, bias=eps[:, 0:1],
                                                 scale=1.0 / groups[g][2]).then_inc(m["qk_sd"], 1)
                        elif what == "turn":
                            c, w, at0 = vg[g]
                            act.wait_ge(m["v_transposed"], g + 1)
                            nc.scalar.activation(tv[:, :, at0:at0 + w * P], pair(mb[3][:, :])[:, :, 0:w * P],
                                                 ACT.Copy).then_inc(m["v_tokens"], 1)
                        elif what == "gates":
                            act.wait_ge(s_y, Y0[n] + M1_CB + 2)
                            nc.scalar.activation(atf[:, 0:6 * SEQ], yc(M1_CQ, 6), ACT.Sigmoid).then_inc(m["gate_sigs"], 1)
                        elif what == "conv":
                            act.wait_ge(s_y, Y0[n] + 8 + 2 * g)
                            nc.scalar.activation(atf[:, 2 * g * SEQ:(2 * g + 1) * SEQ], yc(7 + 2 * g), ACT.Sigmoid
                                                 ).then_inc(m["sigmoids"], 1)
                if kind == "mix1":
                    act.wait_ge(m["v_tokens"], 4)
                    nc.scalar.activation(sgt, tv[:, :, 768:1024], ACT.Sigmoid).then_inc(m["sigmoids"], 1)
                if kind == "even":
                    act.wait_ge(m["ln_sum"], 2)
                    nc.scalar.activation(sd[:, :], mb[2][:, SEQ:2 * SEQ], ACT.Sqrt, bias=eps[:, 0:1],
                                         scale=1.0 / 512).then_inc(m["ln_sd"], 1)
                    act.wait_ge(m["ln_out"], 1)
                    nc.scalar.activation(yc(14, 4), yc(6, 4), ACT.Sigmoid).then_inc(m["ln_sig"], 1)
                    for c in range(4):
                        act.wait_ge(m["mix_sbuf"], c + 1)
                        nc.scalar.activation(hh[:, c, :], yc(6 + c), ACT.Copy).then_inc(m["mix_hi"], 1)
                if kind == "odd":
                    for c in range(4):
                        act.wait_ge(m["mix_psum"], c + 1)
                        nc.scalar.activation(hh[:, 4 + c, :], gb[c][:, 0:SEQ], ACT.Copy, scale=col("ps", c)).then_inc(m["mix_hi"], 1)
                attention(m, kind)
                if kind == "mix1":
                    act.wait_ge(m["mix_psum"], 1)
                    nc.scalar.activation(tmo[:, :, 384:640], pair(gb[2][:, :]), ACT.Copy).then_inc(m["attn_copied"], 1)
                    act.wait_ge(m["stats"], 1)
                    nc.scalar.activation(small[:, 64:80], small[:, 48:64], ACT.Sqrt, bias=eps[:, 0:1]).then_inc(m["stats_sd"], 1)
                    for g, (c, w) in enumerate([(3, 2), (5, 2), (7, 1)]):
                        act.wait_ge(m["mix_psum"], g + 2)
                        nc.scalar.activation(hh[:, c:c + w, :].rearrange("p a b -> p (a b)"),
                                             gb[(0, 1, 3)[g]][:, 0:w * SEQ], ACT.Copy).then_inc(m["mix_hi"], 1)
                for u in range(nin, UNITS[kind]):
                    split_next(U0[n] + u + RING)

            def feed_forward(n, kind, l):
                F, C, U, conv = F0[n], G0[n], U0[n], kind == "ffn1"

                def up(it, j, last):
                    p, i = it * 2 + (F + j), it * 4 + (U + 2 * j)

                    def ahead(k):
                        if last:
                            split_next(i + k + RING)
                        else:
                            b = U + 2 * j + k + RING
                            split(it * 4 + b, b % RING, DC, it * 16 + 16 * (b // RING + 1))

                    if not isinstance(p, int) or p >= 2:
                        act.wait_ge(s_gu, p - 1)
                    act.wait_ge(s_pe, i + 1)
                    gate = gb[2 * j][:, 0:SEQ]
                    if conv:
                        nc.scalar.activation(tap[:, j, :], gate, ACT.Identity,
                                             bias=prm[:, ds(it * 2 + (PRM["cb"] + l * FC + j), 1)],
                                             scale=prm[:, ds(it * 2 + (PRM["cw"] + (3 * l + 1) * FC + j), 1)]).then_inc(s_tap, 1)
                    else:
                        nc.scalar.activation(tap[:, j, :], gate, ACT.Silu).then_inc(s_tap, 1)
                    ahead(0)
                    if conv:
                        act.wait_ge(s_conv, it * 2 + (C + j + 1))
                        nc.scalar.activation(tap[:, j, :], tap[:, j, :], ACT.Gelu).then_inc(s_gelu, 1)
                    ahead(1)
                    act.wait_ge(s_gu, p + 1)
                    nc.scalar.activation(guh[:, ds(it * (2 * SEQ) + j * SEQ, SEQ)], gu[:, j, :], ACT.Copy).then_inc(s_guh, 1)

                for j in range(2):
                    up(0, j, False)
                with act.Fori(1, FC // 2 - 1) as it:
                    for j in range(2):
                        up(it, j, False)
                for j in range(2):
                    up(FC // 2 - 1, j, True)
                with act.Fori(0, 3) as it:
                    for j in range(4):
                        b = U + 2 * FC + RING + j
                        split(it * 4 + b, b % RING, KD, it * 16 + 16 * (b // RING + 1))
                for j in range(4):
                    split_next(U + 2 * FC + 12 + RING + j)

            for i in range(RING):
                split_next(i)
            act.wait_ge(s_ini, 1)
            nc.scalar.activation(par[:, 8:16], par[:, 0:8], ACT.Exp).then_inc(s_inie, 1)
            act.wait_ge(s_eps, 1)
            for n, (kind, l) in enumerate(PHASES):
                norm(n)
                if is_mix[n]:
                    mixer(n, kind, l)
                else:
                    feed_forward(n, kind, l)

        @block.vector
        def _(dve):
            steps = [0]

            def link(ins):
                steps[0] += 1
                ins.then_inc(s_dch, 1)
                dve.wait_ge(s_dch, steps[0])

            def link_second(ins):
                steps[0] += 1
                ins.then_inc(s_dch, 1)
                dve.wait_ge(s_dch, steps[0] - 1)

            def split(i, slot, nt):
                dve.wait_ge(s_hi, i + 1)
                nc.vector.tensor_tensor(wl[:, slot, 0:nt * P], raw[:, slot, 0:nt * P], wh[:, slot, 0:nt * P].bitcast(f32),
                                        ALU.subtract).then_inc(s_lo, 1)

            def split_next(i):
                if i < NU:
                    split(i, i % RING, k_tiles(i))

            def start_values():
                dve.wait_ge(s_prm, 16)
                dve.wait_ge(s_con, 64)
                nc.vector.tensor_copy(msk[:, :, :].rearrange("p a b -> p (a b)"), prf[:, 0:NL * P])
                l0, l1 = prm[:, PRM["lb"]:PRM["lb"] + 2], prm[:, PRM["lb"] + 2:PRM["lb"] + 4]
                link(nc.vector.tensor_tensor(par[:, 16:18], l0, l1, ALU.max))
                nc.vector.tensor_tensor(par[:, 0:2], l0, par[:, 16:18], ALU.subtract)
                nc.vector.tensor_tensor(par[:, 2:4], l1, par[:, 16:18], ALU.subtract)
                prod = qqf[:, 0:192].rearrange("p (a b) -> p a b", a=4)
                link(nc.vector.tensor_tensor(prod, view(row[:, 0:1], [[96, 4], [1, 48]]),
                                             view(row[:, 48:49], [[96, 4], [1, 48]]), ALU.mult))
                nc.vector.reduce_sum(par[:, 4:8], prod, axis=AX.X).then_inc(s_ini, 1)
                dve.wait_ge(s_inie, 1)
                link(nc.vector.tensor_tensor(par[:, 16:18], par[:, 8:10], par[:, 10:12], ALU.add))
                link(nc.vector.reciprocal(par[:, 18:20], par[:, 16:18]))
                nc.vector.tensor_tensor(par[:, 0:2], par[:, 8:10], par[:, 18:20], ALU.mult)
                link(nc.vector.tensor_tensor(par[:, 2:4], par[:, 10:12], par[:, 18:20], ALU.mult))
                link(nc.vector.tensor_tensor(par[:, 4:6], par[:, 0:2], par[:, 2:4], ALU.add))
                link(nc.vector.tensor_tensor(par[:, 20:22], par[:, 0:2], par[:, 0:2], ALU.subtract))
                link(nc.vector.tensor_tensor(par[:, 22:24], par[:, 4:6], par[:, 0:2], ALU.subtract))
                link(nc.vector.tensor_scalar(par[:, 20:24], par[:, 20:24], 0.0, None, ALU.max))
                link(nc.vector.tensor_scalar(par[:, 24:28], par[:, 20:24], -1.0, 1.0, ALU.mult, ALU.add))
                for l in range(2):
                    lam0 = 0.8 - 0.6 * math.exp(-0.3 * l)
                    link(nc.vector.tensor_tensor(par[:, 28 + l:29 + l], par[:, 13 + 2 * l:14 + 2 * l],
                                                 par[:, 12 + 2 * l:13 + 2 * l], ALU.subtract))
                    link(nc.vector.tensor_scalar(par[:, 28 + l:29 + l], par[:, 28 + l:29 + l], lam0, None, ALU.subtract))

            def norm(n):
                dve.wait_ge(s_sd, n + 1)
                link(nc.vector.reciprocal(sd[:, :], sd[:, :]))
                gain, g0 = norm_gain(n)
                for c in range(DC):
                    nc.vector.scalar_tensor_tensor(out=hf[:, c * SEQ:(c + 1) * SEQ], in0=x[:, c * SEQ:(c + 1) * SEQ],
                                                   scalar=col(gain, g0 + c), in1=sd[:, :], op0=ALU.mult,
                                                   op1=ALU.mult).then_inc(s_hf, 1)

            def head_norm(m, g, group):
                c, gains, _ = group
                dve.wait_ge(m["qk_sd"], g + 1)
                w = len(gains) * SEQ
                link(nc.vector.reciprocal(st[:, g % 2, 0:w], st[:, g % 2, 0:w]))
                for k, (name, at0) in enumerate(gains):
                    ins = nc.vector.scalar_tensor_tensor(out=yc(c + k), in0=yc(c + k), scalar=col(name, at0),
                                                         in1=st[:, g % 2, k * SEQ:(k + 1) * SEQ], op0=ALU.mult, op1=ALU.mult)
                ins.then_inc(m["qk_normed"], 1)

            def rope(m, g):
                def both(at0):
                    return view(con[:, at0:at0 + 1], [[0, 2], [1, SEQ]])
                yv, tmp = pair(yc(2 * g, 2)), pair(ptb[:, 0, :])
                dve.wait_ge(m["rotated"], g + 1)
                link(nc.vector.tensor_tensor(tmp, pair(mb[2][:, :]), both(C_SIN), ALU.mult))
                link(nc.vector.tensor_tensor(yv, yv, both(C_COS), ALU.mult))
                nc.vector.tensor_tensor(yv, yv, tmp, ALU.add).then_inc(m["roped"], 1)

            def gates(m, l):
                e = atf[:, 0:6 * SEQ]
                dve.wait_ge(m["gate_sigs"], 1)
                nc.vector.tensor_tensor(yc(M1_CQ, 2), yc(M1_CQ, 2), e[:, 0:2 * SEQ], ALU.mult)
                t0 = tt[0]
                for hp in range(2):
                    lb, rest = par[:, 20 + 2 * l + hp:21 + 2 * l + hp], par[:, 24 + 2 * l + hp:25 + 2 * l + hp]
                    for slot, src in ((0, 4 + hp), (1, 2 + hp), (2, 4 + hp)):
                        last = nc.vector.tensor_scalar(t0[:, 3 * hp + slot, :], e[:, src * SEQ:(src + 1) * SEQ], rest, lb,
                                                       ALU.mult, ALU.add)
                link(last)
                link(nc.vector.tensor_scalar(t0[:, :, :], t0[:, :, :], 1e-20, None, ALU.max))
                for hp in range(2):
                    nc.vector.tensor_scalar(kk[:, hp, :, :], t0[:, 3 * hp + 1:3 * hp + 3, :], -1.0, 1.0, ALU.mult, ALU.add)
                    last = nc.vector.tensor_tensor(qq[:, hp, :, :], t0[:, 3 * hp:3 * hp + 2, :],
                                                   view(yc(M1_CQ + hp)[:, 0:1], [[0, 2], [1, SEQ]]), ALU.mult)
                last.then_inc(m["gates_ready"], 1)

            def convolve(m, c):
                e = atf[:, 2 * c * SEQ:(2 * c + 1) * SEQ]
                taps = PRM["ecw"] + 31 * c
                dve.wait_ge(m["sigmoids"], c + 1)
                if c == 0:
                    nc.vector.memset(qqf[:, 0:30], 0.0)
                link(nc.vector.tensor_tensor(qqf[:, 30:30 + SEQ], yc(6 + 2 * c), e, ALU.mult))
                o, o2 = yc(6 + c), atf[:, (2 * c + 1) * SEQ:(2 * c + 2) * SEQ]
                nc.vector.tensor_scalar(o, qqf[:, 0:SEQ], prm[:, taps:taps + 1], col("ecb", c), ALU.mult, ALU.add)
                link(nc.vector.tensor_scalar(o2, qqf[:, 1:1 + SEQ], prm[:, taps + 1:taps + 2], None, ALU.mult))
                for k in range(2, 31):
                    s = (o, o2)[k % 2]
                    link_second(nc.vector.scalar_tensor_tensor(out=s, in0=qqf[:, k:k + SEQ], scalar=prm[:, taps + k:taps + k + 1],
                                                        in1=s, op0=ALU.mult, op1=ALU.add))
                dve.wait_ge(s_dch, steps[0])
                link(nc.vector.tensor_tensor(o, o, o2, ALU.add))

            def pool_chunk(m, c, n):
                bufs = (qqf, kkf)
                dve.wait_ge(s_y, Y0[n] + 13 + c)
                if c == 0:
                    nc.vector.memset(qqf[:, 0:8], 0.0)
                    nc.vector.memset(kkf[:, 0:8], 0.0)
                link(nc.vector.tensor_copy(qqf[:, 8:8 + SEQ], yc(12 + c)))
                for k in range(c + 1):
                    a, b = bufs[k % 2], bufs[(k + 1) % 2]
                    link(nc.vector.tensor_tensor(b[:, 8:8 + SEQ], a[:, 8:8 + SEQ], a[:, 8 - 2 ** k:8 - 2 ** k + SEQ], ALU.add))
                p = atf[:, c * SEQ:(c + 1) * SEQ]
                link(nc.vector.tensor_tensor(p, bufs[(c + 1) % 2][:, 8:8 + SEQ], con[:, C_INV + c * SEQ:C_INV + (c + 1) * SEQ], ALU.mult))
                nc.vector.tensor_tensor(p, p, yc(12 + c), ALU.subtract).then_inc(m["pooled"], 1)

            def layer_norm(m):
                link(nc.vector.tensor_tensor(acc[:, :], yc(6), yc(7), ALU.add))
                link(nc.vector.tensor_tensor(acc[:, :], acc[:, :], yc(8), ALU.add))
                nc.vector.tensor_tensor(acc[:, :], acc[:, :], yc(9), ALU.add).then_inc(m["ln_operand"], 1)
                dve.wait_ge(m["ln_sum"], 1)
                for c in range(4):
                    last = nc.vector.scalar_tensor_tensor(out=yc(6 + c), in0=mb[2][:, 0:SEQ], scalar=-1.0 / 512, in1=yc(6 + c),
                                                          op0=ALU.mult, op1=ALU.add)
                link(last)
                link(nc.vector.tensor_tensor(yc(14, 4), yc(6, 4), yc(6, 4), ALU.mult))
                link(nc.vector.tensor_tensor(yc(14, 2), yc(14, 2), yc(16, 2), ALU.add))
                nc.vector.tensor_tensor(acc[:, :], yc(14), yc(15), ALU.add).then_inc(m["ln_operand"], 1)
                dve.wait_ge(m["ln_sd"], 1)
                link(nc.vector.reciprocal(sd[:, :], sd[:, :]))
                for c in range(4):
                    last = nc.vector.scalar_tensor_tensor(out=yc(6 + c), in0=yc(6 + c), scalar=col("lng", c), in1=sd[:, :],
                                                          op0=ALU.mult, op1=ALU.mult)
                link(last)
                for c in range(4):
                    last = nc.vector.tensor_scalar(yc(6 + c), yc(6 + c), col("lnb", c), None, ALU.add)
                last.then_inc(m["ln_out"], 1)
                dve.wait_ge(m["ln_sig"], 1)
                for c in range(4):
                    nc.vector.tensor_tensor(yc(6 + c), yc(6 + c), yc(14 + c), ALU.mult).then_inc(m["mix_sbuf"], 1)
                for c in range(4):
                    dve.wait_ge(m["mix_hi"], c + 1)
                    nc.vector.tensor_tensor(hl[:, c, :], yc(6 + c), hh[:, c, :].bitcast(f32), ALU.subtract).then_inc(m["mix_lo"], 1)

            def row_max(m, hs, t):
                h = hs[t]
                for k in range(len(h.rows)):
                    r = row0(hs, t) + k
                    o = 2 * (r % 4)
                    dve.wait_ge(m["scores"], r + 1)
                    s, scale = mb[r % 2][:, :], h.d ** -0.5
                    if h.bias is not None:
                        if r >= 2:
                            dve.wait_ge(m["exps"], r - 1)
                        link(nc.vector.scalar_tensor_tensor(out=st[:, r % 2, :], in0=s, scalar=scale,
                                                            in1=con[:, h.bias:h.bias + 512], op0=ALU.mult, op1=ALU.add))
                        s, scale = st[:, r % 2, :], 1.0
                    link(nc.vector.reduce_max(small[:, 16 + o:18 + o], pair(s), axis=AX.X))
                    if h.sink is not None:
                        link(nc.vector.tensor_scalar(small[:, 16 + o:18 + o], small[:, 16 + o:18 + o],
                                                     row[:, ROW_SINK + h.sink:ROW_SINK + h.sink + 1], None, ALU.max))
                    nc.vector.tensor_scalar(small[:, o:o + 2], small[:, 16 + o:18 + o], -scale, None, ALU.mult).then_inc(m["maxima"], 1)

            def normalise(m, hs, t, l):
                h = hs[t]
                r, nr = row0(hs, t), len(h.rows)
                o = 2 * (r % 4)
                sums = small[:, 8 + o:8 + o + 2 * nr]
                dve.wait_ge(m["exps"], r + nr)
                if h.cnt is not None:
                    link(nc.vector.tensor_tensor(pr[:, r % 4, :], pr[:, r % 4, :], con[:, h.cnt:h.cnt + 512], ALU.mult))
                    link(nc.vector.reduce_sum(sums, pair(pr[:, r % 4, :]), axis=AX.X))
                if h.sink is not None:
                    link(nc.vector.tensor_tensor(sums, sums, small[:, 24 + o:26 + o], ALU.add))
                link(nc.vector.reciprocal(small[:, 80 + o:80 + o + 2 * nr], sums))
                if nr == 2:
                    link(nc.vector.tensor_scalar(small[:, 82 + o:84 + o], small[:, 82 + o:84 + o], par[:, 28 + l:29 + l], None, ALU.mult))
                    for qt in range(2):
                        p2 = pr[:, (r + 1) % 4, qt * SEQ:(qt + 1) * SEQ]
                        last = nc.vector.tensor_scalar(p2, p2, small[:, 82 + o + qt:83 + o + qt], None, ALU.mult)
                    link(last)
                for qt in range(2):
                    p1 = pr[:, r % 4, qt * SEQ:(qt + 1) * SEQ]
                    if nr == 2:
                        last = nc.vector.scalar_tensor_tensor(out=p1, in0=p1, scalar=small[:, 80 + o + qt:81 + o + qt],
                                                              in1=pr[:, (r + 1) % 4, qt * SEQ:(qt + 1) * SEQ], op0=ALU.mult, op1=ALU.add)
                    else:
                        last = nc.vector.tensor_scalar(p1, p1, small[:, 80 + o + qt:81 + o + qt], None, ALU.mult)
                last.then_inc(m["probs"], 1)

            def level(m, v):
                b = v - 1
                w, src, nblk = LEVELS[b], tt[b % 2], SEQ // LEVELS[b]
                dve.wait_ge(m["level_scores"], v + 1)
                if v == 1:
                    dve.wait_ge(m["diag_copied"], 2)
                if b >= 1:
                    dve.wait_ge(m["totals"], b)
                for hp in range(2):
                    qv = view(qq[:, hp, 0, 0:1], [[2 * w, nblk // 2], [SEQ + w, 2], [1, w]])
                    tot = view(src[:, 3 * hp, 1:2], [[2, nblk // 2], [src.shape[-1] - 1, 2], [0, w]])
                    ins = nc.vector.tensor_tensor(qv, qv, tot, ALU.mult)
                ins.then_inc(m["q_up"], 1)
                for k in range(2):
                    nc.vector.copy_predicated(square_blocks(k), view(msk[:, b, 0:1], [[0, 2], [0, 2], [1, P]]),
                                              level_bank(gb[2 * (v % 2) + k])).then_inc(m["level_copied"], 1)

            def attention(m, kind, l):
                hs = heads(kind)
                for t in range(len(hs) + 3):
                    if t < len(hs):
                        row_max(m, hs, t)
                    if 1 <= t <= len(hs):
                        normalise(m, hs, t - 1, l)
                    if kind == "mix1" and 1 <= t <= NL:
                        level(m, t)
                    if 2 <= t < len(hs) + 2 and hs[t - 2].chunk is not None and t % 2 == 1:
                        j = (t - 2) // 2
                        c = hs[t - 2].chunk
                        dve.wait_ge(m["mix_hi"], FIRST[kind] + j + 1)
                        nc.vector.tensor_tensor(hl[:, c, :], mb[3][:, (j % 2) * SEQ:(j % 2 + 1) * SEQ],
                                                hh[:, c, :].bitcast(f32), ALU.subtract).then_inc(m["mix_lo"], 1)

            def out_norms(m, l):
                dve.wait_ge(m["sigmoids"], 1)
                link(nc.vector.tensor_tensor(sgt, sgt, tv[:, :, 768:1024], ALU.mult))
                dve.wait_ge(m["attn_copied"], 5)
                link(nc.vector.tensor_tensor(tms, tmo, tmo, ALU.mult))
                rb = small[:, 48:56].rearrange("p (a b) -> p a b", a=2)
                rc = small[:, 56:64].rearrange("p (a b) -> p a b", a=2)
                for tile in range(2):
                    nc.vector.reduce_sum(rb[:, tile, :], tms[:, tile, 0:384].rearrange("p (h d) -> p h d", h=4), axis=AX.X)
                    last = nc.vector.reduce_sum(rc[:, tile, :], tms[:, tile, 384:640].rearrange("p (h d) -> p h d", h=4), axis=AX.X)
                link(last)
                nc.vector.tensor_scalar(small[:, 48:56], small[:, 48:56], 1.0 / 96, None, ALU.mult)
                nc.vector.tensor_scalar(small[:, 56:64], small[:, 56:64], 1.0 / 64, None, ALU.mult).then_inc(m["stats"], 1)
                dve.wait_ge(m["stats_sd"], 1)
                link(nc.vector.reciprocal(small[:, 64:80], small[:, 64:80]))
                keep = 1.0 - (0.8 - 0.6 * math.exp(-0.3 * l))
                for tile in range(2):
                    for part, w, s0 in ((tmo[:, tile, 0:384], 96, 64 + 4 * tile), (tmo[:, tile, 384:640], 64, 72 + 4 * tile)):
                        pv = part.rearrange("p (h d) -> p h d", h=4)
                        last = nc.vector.tensor_tensor(pv, pv, view(small[:, s0:s0 + 1], [[1, 4], [0, w]]), ALU.mult)
                link(last)
                for tile in range(2):
                    b, c = tmo[:, tile, 0:384], tmo[:, tile, 384:640]
                    nc.vector.scalar_tensor_tensor(out=b, in0=b, scalar=keep, in1=row[:, ROW_SUB + 384 * l:ROW_SUB + 384 * (l + 1)],
                                                   op0=ALU.mult, op1=ALU.mult)
                    last = nc.vector.tensor_tensor(c, c, row[:, ROW_CON + 256 * l:ROW_CON + 256 * (l + 1)], ALU.mult)
                link(last)
                nc.vector.tensor_tensor(tmo[:, :, 384:640], tmo[:, :, 384:640], sgt, ALU.mult).then_inc(m["mix_sbuf"], 1)
                for g, (c, w) in enumerate([(3, 2), (5, 2), (7, 1)]):
                    dve.wait_ge(m["mix_hi"], 3 + g + 1)
                    nc.vector.tensor_tensor(hl[:, c:c + w, :].rearrange("p a b -> p (a b)"), gb[(0, 1, 3)[g]][:, 0:w * SEQ],
                                            hh[:, c:c + w, :].rearrange("p a b -> p (a b)").bitcast(f32),
                                            ALU.subtract).then_inc(m["mix_lo"], 1)

            def mixer(n, kind, l):
                m, nin, plan = M[n], IN_UNITS[kind], beside(kind)
                groups = qk_groups(kind, l)
                for u in range(max(nin, max(plan) + 1)):
                    if u < nin:
                        split_next(U0[n] + u + RING)
                    for what, g in plan.get(u, []):
                        if what == "norm":
                            head_norm(m, g, groups[g])
                        elif what == "rope":
                            rope(m, g)
                        elif what == "gates":
                            gates(m, l)
                        elif what == "conv":
                            convolve(m, g)
                        elif what == "pool":
                            pool_chunk(m, g, n)
                if kind == "even":
                    layer_norm(m)
                if kind == "odd":
                    for c in range(4):
                        dve.wait_ge(m["mix_hi"], c + 1)
                        nc.vector.scalar_tensor_tensor(out=hl[:, 4 + c, :], in0=gb[c][:, 0:SEQ], scalar=col("ps", c),
                                                       in1=hh[:, 4 + c, :].bitcast(f32), op0=ALU.mult, op1=ALU.subtract).then_inc(m["mix_lo"], 1)
                attention(m, kind, l)
                if kind == "mix1":
                    out_norms(m, l)
                for u in range(nin, UNITS[kind]):
                    o = u - nin
                    dve.wait_ge(s_pe, U0[n] + u + 1)
                    xc = x[:, o * SEQ:(o + 1) * SEQ]
                    nc.vector.tensor_tensor(xc, gb[o % 4][:, 0:SEQ], xc, ALU.add).then_inc(s_xo, 1)
                    split_next(U0[n] + u + RING)

            def feed_forward(n, kind, l):
                F, C, U, conv = F0[n], G0[n], U0[n], kind == "ffn1"

                def up(it, j, last):
                    p, i = it * 2 + (F + j), it * 4 + (U + 2 * j)
                    gate, val, t = gb[2 * j], gb[2 * j + 1], tap[:, j, :]

                    def ahead(k):
                        if last:
                            split_next(i + k + RING)
                        else:
                            b = U + 2 * j + k + RING
                            split(it * 4 + b, b % RING, DC)

                    dve.wait_ge(s_tap, p + 1)
                    if conv:
                        w0 = prm[:, ds(it * 2 + (PRM["cw"] + 3 * l * FC + j), 1)]
                        w2 = prm[:, ds(it * 2 + (PRM["cw"] + (3 * l + 2) * FC + j), 1)]
                        nc.vector.scalar_tensor_tensor(out=t[:, 1:SEQ], in0=gate[:, 0:SEQ - 1], scalar=w0, in1=t[:, 1:SEQ],
                                                       op0=ALU.mult, op1=ALU.add).then_inc(s_c1, 1)
                        dve.wait_ge(s_c1, it * 2 + (C + j + 1))
                        nc.vector.scalar_tensor_tensor(out=t[:, 0:SEQ - 1], in0=gate[:, 1:SEQ], scalar=w2, in1=t[:, 0:SEQ - 1],
                                                       op0=ALU.mult, op1=ALU.add).then_inc(s_conv, 1)
                    ahead(0)
                    if conv:
                        dve.wait_ge(s_gelu, it * 2 + (C + j + 1))
                    dve.wait_ge(s_pe, i + 2)
                    if not isinstance(p, int) or p >= 2:
                        dve.wait_ge(s_gul, p - 1)
                    nc.vector.tensor_tensor(gu[:, j, :], val[:, 0:SEQ], t, ALU.mult).then_inc(s_gu, 1)
                    ahead(1)

                def down(it, j, last):
                    b = U + 2 * FC + 2 * j

                    def ahead(k):
                        if last:
                            split_next(it * 4 + b + k + RING)
                        else:
                            split(it * 4 + (b + k + RING), (b + k) % RING, KD)

                    ahead(0)
                    dve.wait_ge(s_pe, it * 4 + (b + 2))
                    xc = x[:, ds(it * (2 * SEQ) + j * SEQ, SEQ)]
                    nc.vector.scalar_tensor_tensor(out=xc, in0=gb[j][:, 0:SEQ], scalar=1.0 if conv else 0.5, in1=xc,
                                                   op0=ALU.mult, op1=ALU.add).then_inc(s_xo, 1)
                    ahead(1)

                for one, trips in ((up, FC // 2 - 1), (down, 3)):
                    for j in range(2):
                        one(0, j, False)
                    with dve.Fori(1, trips) as it:
                        for j in range(2):
                            one(it, j, False)
                    for j in range(2):
                        one(trips, j, True)

            for i in range(RING):
                split_next(i)
            start_values()
            for n, (kind, l) in enumerate(PHASES):
                norm(n)
                if is_mix[n]:
                    mixer(n, kind, l)
                else:
                    feed_forward(n, kind, l)

        @block.tensor
        def _(pe):
            def tiles(i, slot, bank, nt, rhs_h, rhs_l, start, stop, ready=None):
                pe.wait_ge(s_lo, i + 1)
                for k in range(nt):
                    if ready is not None:
                        ready(k)
                    a, b = wh[:, slot, k * P:(k + 1) * P], wl[:, slot, k * P:(k + 1) * P]
                    nc.tensor.matmul(bank, a, rhs_h(k), start=start and k == 0, stop=False)
                    nc.tensor.matmul(bank, a, rhs_l(k), start=False, stop=False)
                    last = nc.tensor.matmul(bank, b, rhs_h(k), start=False, stop=stop and k == nt - 1)
                last.then_inc(s_pe, 1)

            def h_hi(k):
                return hh[:, k, :]

            def h_lo(k):
                return hl[:, k, :]

            def norm(n):
                pe.wait_ge(s_acc, n + 1)
                if n == 0:
                    pe.wait_ge(s_con, 64)
                nc.tensor.matmul(mb[0][:, 0:SEQ], ones, acc[:, :], start=True, stop=True).then_inc(s_ss, 1)

            def level(m, v, n):
                if v == 0:
                    pe.wait_ge(m["gates_ready"], 1)
                    pe.wait_ge(s_y, Y0[n] + IN_UNITS["mix1"])
                else:
                    if v >= 2:
                        pe.wait_ge(m["q_up"], v - 1)
                    if v <= NL:
                        pe.wait_ge(m["k_packed"], v)
                    else:
                        pe.wait_ge(m["k_up"], NL)
                    if v == 2:
                        pe.wait_ge(m["diag_copied"], 2)
                    if v >= 3:
                        pe.wait_ge(m["level_copied"], 2 * (v - 2))
                for i in range(2):
                    for h in range(4):
                        hp, b0 = h // 2, 64 * (h % 2)
                        part = slice(b0, b0 + 64)
                        o = gb[2 * (v % 2) + h % 2][:, (2 * hp + i) * P:(2 * hp + i + 1) * P]
                        ts = slice(i * P, (i + 1) * P)
                        if v == 0:
                            q = y[part, (M1_CQ + hp) * SEQ + i * P:(M1_CQ + hp) * SEQ + (i + 1) * P]
                            nc.tensor.matmul(o, kk[part, hp, 0, ts], q, start=True, stop=False)
                            last = nc.tensor.matmul(o, kk[part, hp, 1, ts], q, start=False, stop=True)
                        elif v <= NL:
                            w = LEVELS[v - 1]
                            dims = [[2 * w, P // (2 * w)], [SEQ + w, 2], [1, w]]
                            last = nc.tensor.matmul(o, kc[v % 2][part, hp, ts],
                                                    view(qq[part, hp, 0, i * P:i * P + 1], dims), start=True, stop=True)
                        else:
                            last = nc.tensor.matmul(o, kk[part, hp, i, ts], qq[part, hp, 1 - i, (1 - i) * P:(2 - i) * P],
                                                    start=True, stop=True)
                last.then_inc(m["level_scores"], 1)

            def scores(m, hs, t):
                for k, (qc, kc, b0) in enumerate(hs[t].rows):
                    r = row0(hs, t) + k
                    part = slice(b0, b0 + hs[t].d)
                    if r >= 2:
                        pe.wait_ge(m["exps"], r - 1)
                    for qt in range(2):
                        last = nc.tensor.matmul(mb[r % 2][:, qt * SEQ:(qt + 1) * SEQ],
                                                y[part, qc * SEQ + qt * P:qc * SEQ + (qt + 1) * P],
                                                y[part, kc * SEQ:(kc + 1) * SEQ], start=True, stop=True)
                    last.then_inc(m["scores"], 1)

            def turn_probs(m, hs, t):
                r = row0(hs, t) % 4
                pe.wait_ge(m["probs"], t + 1)
                if t >= 1:
                    pe.wait_ge(m["probsT"], t)
                for kt in range(2):
                    for qt in range(2):
                        last = nc.tensor.transpose(mb[2][:, kt * SEQ + qt * P:kt * SEQ + (qt + 1) * P],
                                                   pr[:, r, qt * SEQ + kt * P:qt * SEQ + (kt + 1) * P], ident)
                last.then_inc(m["probs_turned"], 1)

            def attend(m, kind, hs, t):
                h = hs[t]
                pe.wait_ge(m["probsT"], t + 1)
                pt = ptb[:, t % 2, :]
                if h.chunk is None:
                    if h.h == 0:
                        pe.wait_ge(m["mix_lo"], 3)
                    else:
                        pe.wait_ge(m["attn_copied"], h.h)
                    for qt in range(2):
                        for kt in range(2):
                            last = nc.tensor.matmul(mb[3][:, qt * SEQ:qt * SEQ + 96], pt[:, kt * SEQ + qt * P:kt * SEQ + (qt + 1) * P],
                                                    tv[:, kt, h.v:h.v + h.vw], start=kt == 0, stop=kt == 1)
                else:
                    j = t // 2
                    if j >= 2 and t % 2 == 0:
                        pe.wait_ge(m["mix_lo"], FIRST[kind] + j - 1)
                    for kt in range(2):
                        last = nc.tensor.matmul(mb[3][h.base:h.base + 64, (j % 2) * SEQ:(j % 2 + 1) * SEQ],
                                                tv[:, kt, h.v:h.v + h.vw], pt[:, kt * SEQ:(kt + 1) * SEQ], start=kt == 0, stop=kt == 1)
                last.then_inc(m["attn_out"], 1)

            def attention(m, kind, n):
                hs = heads(kind)
                for t in range(len(hs) + 3):
                    if t < len(hs):
                        scores(m, hs, t)
                    if kind == "mix1" and t <= NL + 1:
                        level(m, t, n)
                    if 1 <= t <= len(hs):
                        turn_probs(m, hs, t - 1)
                    if 2 <= t < len(hs) + 2:
                        attend(m, kind, hs, t - 2)

            def mixer(n, kind, l):
                m, nin, plan = M[n], IN_UNITS[kind], beside(kind)
                groups, vg = qk_groups(kind, l), V_GROUPS[kind]
                for u in range(max(nin, max(plan) + 1)):
                    if u < nin:
                        if u >= 4:
                            pe.wait_ge(s_y, Y0[n] + u - 3)
                        i = U0[n] + u
                        tiles(i, i % RING, gb[u % 4][:, 0:SEQ], DC, h_hi, h_lo, True, True,
                              (lambda k: pe.wait_ge(s_hl, DC * n + k + 1)) if u == 0 else None)
                    for what, g in plan.get(u, []):
                        if what == "norm":
                            w = len(groups[g][1]) * SEQ
                            pe.wait_ge(m["qk_squared"], g + 1)
                            if g >= 2:
                                pe.wait_ge(m["qk_sd"], g - 1)
                            nc.tensor.matmul(mb[g % 2][:, 0:w], con[:, C_BLK:C_BLK + P], sq[:, 0:w], start=True,
                                             stop=True).then_inc(m["qk_sums"], 1)
                        elif what == "rope":
                            pe.wait_ge(m["qk_normed"], g + 1)
                            if g:
                                pe.wait_ge(m["roped"], g)
                            nc.tensor.matmul(mb[2][:, :], con[:, C_PERM:C_PERM + P], yc(2 * g, 2), start=True,
                                             stop=True).then_inc(m["rotated"], 1)
                        elif what == "turn":
                            c, w, _ = vg[g]
                            pe.wait_ge(s_y, Y0[n] + c + w)
                            if g:
                                pe.wait_ge(m["v_tokens"], g)
                            for cc in range(w):
                                for tile in range(2):
                                    last = nc.tensor.transpose(mb[3][:, tile * SEQ + cc * P:tile * SEQ + (cc + 1) * P],
                                                               y[:, (c + cc) * SEQ + tile * P:(c + cc) * SEQ + (tile + 1) * P], ident)
                            last.then_inc(m["v_transposed"], 1)
                pe.wait_ge(m["v_tokens"], len(vg))
                pe.wait_ge(m["qk_normed"], len(groups))
                if kind == "mix1":
                    pe.wait_ge(m["roped"], 2)
                if kind == "even":
                    for k in range(2):
                        pe.wait_ge(m["ln_operand"], k + 1)
                        nc.tensor.matmul(mb[2][:, k * SEQ:(k + 1) * SEQ], ones, acc[:, :], start=True, stop=True).then_inc(m["ln_sum"], 1)
                    pe.wait_ge(m["ln_sd"], 1)
                if kind == "odd":
                    pe.wait_ge(s_y, Y0[n] + nin)
                    for c in range(4):
                        pe.wait_ge(m["pooled"], c + 1)
                        nc.tensor.matmul(gb[c][:, 0:SEQ], poolw[:, c, :], atf[:, c * SEQ:(c + 1) * SEQ], start=True,
                                         stop=True).then_inc(m["mix_psum"], 1)
                attention(m, kind, n)
                if kind == "mix1":
                    pe.wait_ge(m["diag_copied"], 4)
                    pe.wait_ge(m["level_copied"], 2 * NL)
                    for tile in range(2):
                        for h in range(4):
                            for s in range(2):
                                last = nc.tensor.matmul(gb[2][:, tile * SEQ + 64 * h:tile * SEQ + 64 * (h + 1)],
                                                        at[:, s, h, tile * P:(tile + 1) * P], tv[:, s, 512 + 64 * h:512 + 64 * (h + 1)],
                                                        start=s == 0, stop=s == 1)
                    last.then_inc(m["mix_psum"], 1)
                    pe.wait_ge(m["mix_sbuf"], 1)
                    for g, (c, w) in enumerate([(3, 2), (5, 2), (7, 1)]):
                        for cc in range(w):
                            for tile in range(2):
                                at0 = (c - 3 + cc) * P
                                last = nc.tensor.transpose(gb[(0, 1, 3)[g]][:, cc * SEQ + tile * P:cc * SEQ + (tile + 1) * P],
                                                           tmo[:, tile, at0:at0 + P], ident)
                        last.then_inc(m["mix_psum"], 1)
                pe.wait_ge(m["mix_lo"], MIX_GROUPS[kind])
                for u in range(nin, UNITS[kind]):
                    i, o = U0[n] + u, u - nin
                    if o >= 4:
                        pe.wait_ge(s_xo, DC * n + o - 3)
                    tiles(i, i % RING, gb[o % 4][:, 0:SEQ], DC, h_hi, h_lo, True, True)

            def feed_forward(n, kind, l):
                F, U = F0[n], U0[n]

                def up(it, j, first, banks=True):
                    for k in range(2):
                        i = it * 4 + (U + 2 * j + k)
                        if not first and k == 0:
                            pe.wait_ge(s_gu, it * 2 + (F + j - 1))
                        tiles(i, (U + 2 * j + k) % RING, gb[2 * j + k][:, 0:SEQ], DC, h_hi, h_lo, True, True,
                              (lambda k: pe.wait_ge(s_hl, DC * n + k + 1)) if first and j + k == 0 else None)

                for j in range(2):
                    up(0, j, True)
                with pe.Fori(1, FC // 2) as it:
                    for j in range(2):
                        up(it, j, False)

                def down(it, j, first):
                    for k in range(2):
                        b = U + 2 * FC + 2 * j + k
                        if not first and k == 0:
                            pe.wait_ge(s_xo, it * 2 + (DC * n + j - 1))
                        tiles(it * 4 + b, b % RING, gb[j][:, 0:SEQ], KD,
                              lambda c: guh[:, (k * KD + c) * SEQ:(k * KD + c + 1) * SEQ],
                              lambda c: gul[:, (k * KD + c) * SEQ:(k * KD + c + 1) * SEQ], k == 0, k == 1,
                              (lambda c: pe.wait_ge(s_gul, F + k * KD + c + 1)) if first and j == 0 else None)

                for j in range(2):
                    down(0, j, True)
                with pe.Fori(1, 4) as it:
                    for j in range(2):
                        down(it, j, False)

            for n, (kind, l) in enumerate(PHASES):
                norm(n)
                if is_mix[n]:
                    mixer(n, kind, l)
                else:
                    feed_forward(n, kind, l)


def units_of(w):
    k, n = w.shape
    return w.reshape(k // P, P, n // P, P).transpose(2, 1, 0, 3).reshape(n // P, P, k)


def up_units(gate, val):
    g, v = units_of(gate), units_of(val)
    return np.stack([g, v], 1).reshape(2 * g.shape[0], P, -1)


def down_units(w):
    u = units_of(w)
    return u.reshape(DC, P, 2, KD * P).transpose(0, 2, 1, 3).reshape(2 * DC, P, KD * P)


def pad_to(a, n, axis):
    shape = list(a.shape)
    shape[axis] = n - shape[axis]
    return np.concatenate([a, np.zeros(shape, a.dtype)], axis)


def per_chunk(v):
    return v.reshape(-1, P).T


def kernel(**inputs):
    import concourse.bacc as _bacc
    from concourse import mybir as _mybir
    from concourse.bass_utils import run_bass_kernel_spmd as _run

    a = {k: np.asarray(v) for k, v in inputs.items()}
    ff = FC * P

    def m1_columns(w):
        c = np.split(w, np.cumsum([384, 128, 128, 384, 384, 384, 256, 256, 256, 256]), axis=1)
        aq, ak, av, bq, bk, bv, cq, cf, cb, cv, cg = c
        aq = aq.reshape(D, 2, 3, 64).transpose(0, 2, 1, 3).reshape(D, 384)
        bq, bk = (pad_to(t.reshape(D, 8, 48), 64, 2).reshape(D, 512) for t in (bq, bk))
        return np.concatenate([aq, ak, bq, bk, cq, cf, cb, av, bv, cv, cg], 1)

    def m1_rows(w):
        return np.concatenate([w[:384].reshape(2, 3, 64, D).transpose(1, 0, 2, 3).reshape(384, D), w[384:]], 0)

    def ev_columns(w):
        val, gate, q, k, v = np.split(w, np.cumsum([512, 512, 512, 128]), axis=1)
        q = q.reshape(D, 2, 4, 64).transpose(0, 2, 1, 3).reshape(D, 512)
        vg = np.stack([val.reshape(D, 4, P), gate.reshape(D, 4, P)], 2).reshape(D, 1024)
        return np.concatenate([q, k, v, vg], 1)

    def ev_rows(w):
        return np.concatenate([w[:512], w[512:].reshape(2, 4, 64, D).transpose(1, 0, 2, 3).reshape(512, D)], 0)

    wa, wb = [], []
    for kind, l in PHASES:
        if kind == "mix1":
            wa += [units_of(m1_columns(a["w_in"][l])), units_of(m1_rows(a["w_out"][l]))]
        elif kind == "even":
            wa += [units_of(ev_columns(a["ev_w_in_2"][0])), units_of(ev_rows(a["ev_w_out_2"][0]))]
        elif kind == "odd":
            wa += [units_of(a["od_w_in_2"][0]), units_of(a["od_w_out_2"][0])]
        elif kind == "ffn1":
            wa.append(up_units(a["w_up"][l][:, :ff], a["w_up"][l][:, ff:]))
            wb.append(down_units(a["w_down"][l]))
        else:
            i, j = l // 2, l % 2
            wa.append(up_units(pad_to(a["ffn_w_gate_2"][i, j], ff, 1), pad_to(a["ffn_w_up_2"][i, j], ff, 1)))
            wb.append(down_units(pad_to(a["ffn_w_down_2"][i, j], ff, 0)))

    def both_heads(g):
        return np.concatenate([g, g])[:, None]

    def both_halves(g):
        return both_heads(pad_to(g, 64, 0))

    prm = np.concatenate(
        [per_chunk(a["attn_norm"]), per_chunk(a["ffn_norm"]), per_chunk(a["norm_g_2"]), per_chunk(a["conv_w"]),
         per_chunk(a["conv_b"])]
        + [both_heads(a["a_q_norm"][l]) for l in range(2)] + [both_heads(a["a_k_norm"][l]) for l in range(2)]
        + [both_halves(a["b_q_norm"][l]) for l in range(2)] + [both_halves(a["b_k_norm"][l]) for l in range(2)]
        + [per_chunk(a["c_lb_logits"]), a["ev_conv_w_2"][0].reshape(31, 4, P).transpose(2, 1, 0).reshape(P, 124),
           per_chunk(a["ev_conv_b_2"]), per_chunk(a["ev_ln_g_2"]), per_chunk(a["ev_ln_b_2"]),
           both_heads(a["ev_q_norm_g_2"][0]), both_heads(a["ev_k_norm_g_2"][0]), both_heads(a["od_q_norm_g_2"][0]),
           both_heads(a["od_k_norm_g_2"][0]), per_chunk(a["od_pool_scale_2"])], 1)
    row = np.concatenate([a["b_lambda"].ravel(), a["b_sub_norm"].ravel(), a["c_out_norm"].ravel(), a["ev_sinks_2"].ravel()])
    const, mask = shape_constants()
    ins = {
        "x": a["x"][0].T.reshape(DC, P, SEQ).transpose(1, 0, 2).reshape(P, DC * SEQ),
        "wa": np.concatenate(wa, 0), "wb": np.concatenate(wb, 0), "prm": prm, "row": row[None, :],
        "const": const, "mask": mask, "pool_w": a["od_pool_w_2"][0].transpose(1, 0, 2),
    }
    ins = {f"in_{k}": np.ascontiguousarray(v) for k, v in ins.items()}
    nc = _bacc.Bacc("TRN2", target_bir_lowering=False, num_devices=1)
    args = [nc.dram_tensor(k, v.shape, _mybir.dt.from_np(v.dtype), kind="ExternalInput").ap() for k, v in ins.items()]
    args.append(nc.dram_tensor("out_x", (P, DC * SEQ), _mybir.dt.float32, kind="ExternalOutput").ap())
    build_program(nc, *args)
    r = _run(nc, [ins], core_ids=[0])
    y = r.results[0]["out_x"]
    return y.reshape(P, DC, SEQ).transpose(1, 0, 2).reshape(D, SEQ).T[None]
```

```python
import math

import numpy as np

P = 128
D = 1024
SEQ = 256
DC = D // P
FC = 22
KD = FC // 2
RING = 4
EPS = 1e-6

PHASES = [("mix1", 0), ("ffn1", 0), ("mix1", 1), ("ffn1", 1), ("ffn2", 0), ("even", 0),
          ("ffn2", 1), ("ffn2", 2), ("odd", 0), ("ffn2", 3)]
IN_UNITS = {"mix1": 26, "even": 14, "odd": 16}
UNITS = {"mix1": 26 + 8, "even": 14 + 8, "odd": 16 + 8, "ffn1": 2 * FC + 16, "ffn2": 2 * FC + 16}

M1_AQ, M1_AK, M1_AV, M1_CQ, M1_CF, M1_CB, M1_CG, M1_CV, M1_BV, M1_B = 0, 3, 4, 5, 7, 9, 11, 13, 15, 18
A_ORDER = [0, 3, 1, 4, 2, 5]

PRM = {}


def _prm_layout():
    at = 0
    for name, n in [("n1", 2 * 8), ("nf", 2 * 8), ("n2", 6 * 8), ("cw", 2 * 3 * FC), ("cb", 2 * FC), ("aq", 2), ("ak", 2),
                    ("bq", 2), ("bk", 2), ("lb", 4), ("ecw", 31 * 4), ("ecb", 4), ("lng", 4), ("lnb", 4),
                    ("eq", 1), ("ek", 1), ("oq", 1), ("ok", 1), ("ps", 4)]:
        PRM[name] = at
        at += n
    return at


NPRM = _prm_layout()
ROW_LAM, ROW_SUB, ROW_CON, ROW_SINK, NROW = 0, 384, 384 + 768, 384 + 768 + 512, 384 + 768 + 512 + 8
C_ID, C_PERM, C_ONE, C_BLK, C_COS, C_SIN, C_INV = 0, 128, 256, 384, 512, 768, 1024
NCONST = C_INV + 4 * 16
BIAS = {"mix1": 0, "even": 512, "odd": 1024}
NBIAS = {"mix1": 512, "even": 512, "odd": 1024}
LEVELS = [1, 2, 4, 8, 16, 32, 64]


def shape_constants():
    c = np.zeros((P, NCONST), np.float32)
    p = np.arange(P)
    c[:, C_ID:C_ID + P] = np.eye(P)
    c[p, C_PERM + (p ^ 16)] = 1.0
    c[:, C_ONE:C_ONE + P] = 1.0
    c[:, C_BLK:C_BLK + P] = (p[:, None] // 64) == (p[None, :] // 64)
    t = np.arange(SEQ)
    row, col = t // 64, t % 64
    half = 16
    inv = (np.float32(10000.0) ** (-np.arange(0, 32, 2, dtype=np.float32) / np.float32(32))).astype(np.float32)
    axis = (p % 64) // 32
    pos = np.where(axis[:, None] == 0, row[None, :], col[None, :]).astype(np.float32)
    ang = (pos * inv[p % half][:, None]).astype(np.float32)
    c[:, C_COS:C_COS + SEQ] = np.cos(ang)
    c[:, C_SIN:C_SIN + SEQ] = np.sin(ang) * np.where((p % 32) < half, -1.0, 1.0)[:, None]
    q = (np.arange(2)[None, :, None] * P + p[:, None, None])
    k = t[None, None, :]
    d = (q - k)
    b = np.zeros((P, 2048), np.float32)
    b[:, 0:512] = np.abs(d).reshape(P, 512)
    b[:, 512:1024] = np.where((d >= 0) & (d <= 127), 0.0, -1e30).reshape(P, 512)
    count = ((d >= 0) & (d <= 128)).astype(int) + ((d >= 0) & (d % 4 == 0)) + ((d >= 0) & (d % 16 == 0))
    b[:, 1024:1536] = np.where(count > 0, 0.0, -1e30).reshape(P, 512)
    b[:, 1536:2048] = count.reshape(P, 512)
    for g, w in enumerate((2, 4, 8, 16)):
        c[:, C_INV + 16 * g:C_INV + 16 * (g + 1)] = 1.0 / np.minimum(t[:16] + 1, w)
    m = np.zeros((P, len(LEVELS), P), np.float32)
    for n, w in enumerate(LEVELS):
        m[:, n, :] = ((p[:, None] // (2 * w)) == (p[None, :] // (2 * w))) & ((p[:, None] // w) != (p[None, :] // w))
    return c, b, m.reshape(P, -1)


class Head:

    def __init__(self, rows, d, bias, v, vw, chunk, base, cnt=None, sink=None, h=0):
        self.rows, self.d, self.bias, self.v, self.vw = rows, d, bias, v, vw
        self.chunk, self.base, self.cnt, self.sink, self.h = chunk, base, cnt, sink, h


def build_program(nc, xin, wa, wb, prm_d, row_d, const_d, bias_d, mask_d, pw_d, out):
    import concourse.bass as bass
    from concourse import mybir
    from contextlib import ExitStack

    f32, r32, u8 = mybir.dt.float32, mybir.dt.float32r, mybir.dt.uint8
    ACT, ALU, AX = mybir.ActivationFunctionType, mybir.AluOpType, mybir.AxisListType
    AP, ds = bass.AP, bass.ds
    NPH = len(PHASES)
    U0 = [sum(UNITS[k] for k, _ in PHASES[:n]) for n in range(NPH + 1)]
    NU = U0[-1]
    is_mix = [k in IN_UNITS for k, _ in PHASES]
    F0 = [FC * sum(not m for m in is_mix[:n]) for n in range(NPH)]
    G0 = [FC * sum(k == "ffn1" for k, _ in PHASES[:n]) for n in range(NPH)]
    Y0 = [sum(IN_UNITS.get(k, 0) for k, _ in PHASES[:n]) for n in range(NPH)]

    def k_tiles(i):
        n = max(n for n in range(NPH) if U0[n] <= i)
        return KD if not is_mix[n] and i - U0[n] >= 2 * FC else DC

    ctx = ExitStack()
    with ctx:
        def sb(name, shape, dt=f32, c=ctx):
            return c.enter_context(nc.sbuf_tensor(name, shape, dt))

        def sem(name):
            return ctx.enter_context(nc.semaphore(name))

        raw = sb("raw", [P, RING, KD * P])
        wh = sb("wh", [P, RING, KD * P], r32)
        wl = sb("wl", [P, RING, KD * P], r32)
        x = sb("x", [P, DC * SEQ])
        hh = sb("hh", [P, DC * SEQ], r32)
        hl = sb("hl", [P, DC * SEQ], r32)
        mh = sb("mh", [P, DC * SEQ], r32)
        ml = sb("ml", [P, DC * SEQ], r32)
        prm = sb("prm", [P, NPRM])
        row = sb("row", [P, NROW])
        con = sb("con", [P, NCONST])
        tab = sb("tab", [P, 1024])
        msk = sb("msk", [P, len(LEVELS), P], u8)
        poolw = sb("poolw", [P, 4, P])
        sq = sb("sq", [P, 2 * SEQ])
        acc = sb("acc", [P, SEQ])
        rstd = sb("rstd", [P, SEQ])
        tap = sb("tap", [P, 2, SEQ])
        gu = sb("gu", [P, 2, SEQ])
        gs = sb("gs", [P, 2, SEQ + 2])
        eps = sb("eps", [P, 1])
        par = sb("par", [P, 32])
        small = sb("small", [P, 96])
        with ExitStack() as turn:
            guh = sb("guh", [P, FC * SEQ], r32, turn)
            gul = sb("gul", [P, FC * SEQ], r32, turn)
        y = sb("y", [P, 26 * SEQ])
        tv = sb("tv", [P, 2, 1024])
        pr = sb("pr", [P, 6, 2 * SEQ])
        ptb = sb("ptb", [P, 2, 2 * SEQ])
        qq = sb("qq", [P, 2, 2, SEQ])
        kk = sb("kk", [P, 2, 2, SEQ])
        kc = (tap, gu)
        tt0 = sb("tt0", [P, 6, SEQ])
        at = sb("at", [P, 2, 4, SEQ])

        gb = [ctx.enter_context(nc.psum_tensor(f"gb{n}", [P, 512], f32)) for n in range(4)]
        mb = [ctx.enter_context(nc.psum_tensor(f"mb{n}", [P, 512], f32)) for n in range(4)]

        atf = at[:, :, :, :].rearrange("p a b c -> p (a b c)")
        prf = pr[:, :, :].rearrange("p a b -> p (a b)")
        qqf = qq[:, :, :, :].rearrange("p a b c -> p (a b c)")
        kkf = kk[:, :, :, :].rearrange("p a b c -> p (a b c)")
        tmo = y[:, 7 * SEQ:12 * SEQ].rearrange("p (a b) -> p a b", a=2)
        tms = y[:, 0:5 * SEQ].rearrange("p (a b) -> p a b", a=2)
        tt = (tt0, y[:, 0:3 * SEQ].rearrange("p (a b) -> p a b", a=6))
        ident = con[:, C_ID:C_ID + P]
        ones = con[:, C_ONE:C_ONE + P]

        def yc(c, n=1):
            return y[:, c * SEQ:(c + n) * SEQ]

        def pair(ap):
            return ap.rearrange("p (a b) -> p a b", a=2)

        def mc(buf, c, n=1):
            return buf[:, c * SEQ:(c + n) * SEQ]

        def every_other(c):
            return view(y[:, c * SEQ:c * SEQ + 1], [[2 * SEQ, 4], [1, SEQ]])

        def col(name, n=0):
            return prm[:, PRM[name] + n:PRM[name] + n + 1]

        def view(ap, dims):
            return AP(ap.tensor, ap.offset, [list(ap.ap[0])] + dims)

        def level_bank(bank):
            return bank[:, :].rearrange("p (a b c) -> p a b c", a=2, b=2)

        def square_blocks(b):
            return view(at[:, 0, b, 0:1], [[2 * SEQ, 2], [4 * SEQ + P, 2], [1, P]])

        def cross_blocks(b):
            return view(at[:, 0, b, P:P + 1], [[2 * SEQ, 2], [4 * SEQ - P, 2], [1, P]])

        s_raw = [sem(f"raw_loaded{n}") for n in range(RING)]
        s_x0, s_prm, s_con, s_out = sem("x_loaded"), sem("params_loaded"), sem("consts_loaded"), sem("out_written")
        s_hi, s_lo, s_pe = sem("w_hi_ready"), sem("w_lo_ready"), sem("unit_multiplied")
        s_y, s_xo = sem("chunk_projected"), sem("x_updated")
        s_tap, s_c1, s_conv, s_gelu = sem("tap_ready"), sem("second_tap"), sem("conv_ready"), sem("gelu_ready")
        s_gu, s_guh, s_gul = sem("hidden_ready"), sem("hidden_hi_ready"), sem("hidden_lo_ready")
        s_acc, s_ss, s_sd = sem("squares_summed"), sem("x_sum_ready"), sem("x_sd_ready")
        s_hh, s_hl, s_rs = sem("h_hi_ready"), sem("h_lo_ready"), sem("rstd_ready")
        s_tab, s_gs, s_up = sem("tables_loaded"), sem("gate_normed"), sem("act_scaled")
        s_dch, s_pch = sem("vector_step"), sem("gpsimd_step")
        s_eps, s_ini, s_inie = sem("eps_set"), sem("start_values"), sem("start_exps")

        NAMES = ("qk_squared qk_sums qk_sd qk_normed rotated roped v_transposed v_tokens scores maxima exps "
                 "probs probs_turned probsT attn_out attn_copied mix_psum mix_sbuf mix_hi mix_lo").split()
        OWN = {"mix1": ("gate_sigs gates_ready k_packed level_scores diag_copied level_copied totals q_up k_up stats "
                        "stats_sd c_copied").split(),
               "even": "sigmoids ln_operand ln_sum ln_sd ln_out ln_sig".split(), "odd": ["pooled"]}
        M = {n: {w: sem(f"{k}{l}_{w}") for w in NAMES + OWN[k]}
             for n, (k, l) in enumerate(PHASES) if k in IN_UNITS}

        def norm_gain(n):
            kind, l = PHASES[n]
            return {"mix1": ("n1", 8 * l), "ffn1": ("nf", 8 * l), "even": ("n2", 8), "odd": ("n2", 32),
                    "ffn2": ("n2", 8 * (0, 2, 3, 5)[l % 4])}[kind]

        def qk_groups(kind, l):
            if kind == "mix1":
                return ([(0, [("aq", l), ("aq", l)], 64), (2, [("aq", l), ("ak", l)], 64)] +
                        [(M1_B + 2 * h, [("bq", l), ("bk", l)], 48) for h in range(4)])
            if kind == "even":
                return [(9, [("ek", 0), ("eq", 0)], 64), (11, [("eq", 0), ("eq", 0)], 64), (13, [("eq", 0)], 64)]
            return [(4 + 2 * c, [("oq", 0), ("ok", 0)], 64) for c in range(4)]

        V_GROUPS = {"mix1": [(M1_AV, 1, 0), (M1_CG, 2, 768), (M1_CV, 2, 512), (M1_BV, 2, 128), (M1_BV + 2, 1, 384)],
                    "even": [(8, 1, 0)], "odd": [(0, 2, 0), (2, 2, 256)]}

        def heads(kind):
            if kind == "mix1":
                return ([Head([(M1_AQ + h % 3, M1_AK, 64 * (h // 3))], 64, None, 64 * (h // 3), 64, h % 3, 64 * (h // 3))
                         for h in A_ORDER] +
                        [Head([(M1_B + 2 * h, M1_B + 2 * h + 1, 0), (M1_B + 2 * h, M1_B + 2 * h + 1, 64)], 48,
                              -(2.0 ** (-2.0 * (h + 1))) * 48 ** 0.5, 128 + 96 * h, 96, None, 0, h=h) for h in range(4)])
            if kind == "even":
                return [Head([(10 + c, 9, 64 * g)], 64, 1.0, 64 * g, 64, 4 + c, 64 * g, sink=c + 4 * g)
                        for c in range(4) for g in range(2)]
            return [Head([(4 + 2 * (h // 2), 5 + 2 * (h // 2), 64 * (h % 2))], 64, 1.0, 64 * h, 64, h // 2, 64 * (h % 2), cnt=True)
                    for h in range(8)]

        def row0(hs, t):
            return sum(len(h.rows) for h in hs[:t])

        NL = len(LEVELS)
        W = {"mix1": [(1, "sqr", 0), (2, "sum", 0), (2, "norm", 0), (3, "sqr", 1), (4, "sum", 1), (4, "norm", 1),
                      (5, "rotate", 0), (5, "rope", 0), (6, "turn", 0), (7, "rotate", 1), (7, "rope", 1),
                      (9, "attn", 0), (10, "attn", 1), (11, "attn", 2), (12, "attn", 3), (13, "attn", 4), (13, "gates", 0),
                      (14, "attn", 5), (16, "level", 0), (17, "turn", 1), (17, "level", 1), (18, "turn", 2),
                      (18, "level", 2), (19, "level", 3), (19, "turn", 3), (20, "level", 4), (20, "turn", 4), (20, "sqr", 2),
                      (21, "level", 5), (21, "sum", 2), (21, "norm", 2), (22, "level", 6), (22, "sqr", 3), (23, "level", 7),
                      (23, "sum", 3), (23, "attn", 6), (23, "norm", 3), (24, "level", 8), (24, "sqr", 4), (25, "sum", 4),
                      (25, "norm", 4), (25, "attn", 7), (25, "sqr", 5), (26, "cout", 0), (26, "sum", 5), (26, "norm", 5)] +
                     [(26, "attn", t) for t in range(8, 14)] + [(26, "post", 0)],
             "even": [(1, "sig", 0), (2, "conv", 0), (3, "sig", 1), (3, "conv", 1), (4, "conv", 2), (5, "sig", 2), (5, "conv", 3),
                      (6, "conv", 4), (7, "sig", 3), (7, "conv", 5), (8, "conv", 6), (9, "turn", 0), (9, "conv", 7),
                      (10, "conv", 8), (11, "sqr", 0), (11, "conv", 9), (12, "sum", 0), (12, "norm", 0), (12, "sqr", 1),
                      (12, "conv", 10), (13, "attn", 0), (13, "sum", 1), (13, "norm", 1), (13, "sqr", 2), (13, "conv", 11),
                      (14, "attn", 1), (14, "sum", 2), (14, "norm", 2), (14, "attn", 2), (14, "conv", 12), (14, "attn", 3),
                      (14, "attn", 4), (14, "conv", 13), (14, "attn", 5), (14, "attn", 6), (14, "conv", 14), (14, "attn", 7),
                      (14, "attn", 8), (14, "conv", 15), (14, "attn", 9), (14, "attn", 10), (14, "attn", 11), (14, "ln", 0)],
             "odd": [(2, "turn", 0), (4, "turn", 1), (5, "sqr", 0), (6, "sum", 0), (6, "norm", 0), (7, "sqr", 1), (8, "sum", 1),
                     (8, "norm", 1), (8, "attn", 0), (9, "sqr", 2), (9, "attn", 1), (10, "sum", 2), (10, "norm", 2),
                     (10, "attn", 2), (11, "sqr", 3), (11, "attn", 3), (12, "sum", 3), (12, "norm", 3), (12, "attn", 4),
                     (13, "attn", 5), (14, "attn", 6), (14, "pool", 0), (15, "attn", 7), (15, "pool", 1), (16, "attn", 8),
                     (16, "pool", 2), (16, "attn", 9), (16, "pool", 3), (16, "attn", 10), (16, "attn", 11)]}

        def outputs(kind, what, t):
            if what == "attn":
                hs = heads(kind)
                return 1 if 4 <= t < len(hs) + 4 and hs[t - 4].chunk is not None and t % 2 == 1 else 0
            return {"post": 3, "ln": 4, "pool": 1}.get(what, 0)

        def before(kind, what, t):
            n = 0
            for _, w, k in W[kind]:
                if (w, k) == (what, t):
                    return n
                n += outputs(kind, w, k)

        BIASED = {k: [hd.bias is not None for hd in heads(k) for _ in hd.rows] for k in W}
        MISC = mb[2]

        def bank_of(kind, u):
            return u % 4 if kind != "mix1" or u < 13 else u % 2

        def freed_by(kind, u):
            return max([v + 1 for v in range(u) if bank_of(kind, v) == bank_of(kind, u)] + [0])

        def plan(kind, u):
            return [(what, t) for step, what, t in W[kind] if step == u]

        def row_owner(hs, r):
            return max(t for t in range(len(hs)) if row0(hs, t) <= r)

        def group_of(kind, l, c):
            return max(g for g, (c0, _, _) in enumerate(qk_groups(kind, l)) if c0 <= c)

        T0 = [16 * sum(is_mix[:n + 1]) for n in range(NPH)]

        MIX_OUT = {k: sum(outputs(k, w, t) for _, w, t in W[k]) for k in W}

        block = ctx.enter_context(nc.Block())

        @block.sync
        def _(sp):
            sp.dma_start(x[:, :], xin).then_inc(s_x0, 16)
            sp.dma_start(prm[:, :], prm_d).then_inc(s_prm, 16)
            na = nb = 0

            def load(i, slot, src, width):
                if not isinstance(i, int) or i >= RING:
                    sp.wait_ge(s_lo, i - (RING - 1))
                sp.dma_start(raw[:, slot, 0:width], src).then_inc(s_raw[slot], 16)

            for n, (kind, l) in enumerate(PHASES):
                if is_mix[n]:
                    if n:
                        sp.wait_ge(s_xo, DC * (n - 1) + 1)
                    sp.dma_start(tab[:, 0:NBIAS[kind]], bias_d[:, BIAS[kind]:BIAS[kind] + NBIAS[kind]]).then_inc(s_tab, 16)
                    for u in range(UNITS[kind]):
                        i = U0[n] + u
                        load(i, i % RING, wa[na + u, :, :], DC * P)
                    na += UNITS[kind]
                else:
                    with sp.Fori(0, FC // 2) as it:
                        for j in range(4):
                            i = U0[n] + j
                            load(it * 4 + i, i % RING, AP(wa.tensor, it * (4 * P * DC * P) + (na + j) * (P * DC * P),
                                                          [[DC * P, P], [1, DC * P]]), DC * P)
                    na += 2 * FC
                    with sp.Fori(0, 4) as it:
                        for j in range(4):
                            i = U0[n] + 2 * FC + j
                            load(it * 4 + i, i % RING, AP(wb.tensor, it * (4 * P * KD * P) + (nb + j) * (P * KD * P),
                                                          [[KD * P, P], [1, KD * P]]), KD * P)
                    nb += 16
            for c in range(DC):
                sp.wait_ge(s_xo, DC * (NPH - 1) + c + 1)
                sp.dma_start(out[:, c * SEQ:(c + 1) * SEQ], x[:, c * SEQ:(c + 1) * SEQ]).then_inc(s_out, 16)
            sp.wait_ge(s_out, 16 * DC)

        @block.gpsimd
        def _(pool):
            steps = [0]

            def link(ins):
                steps[0] += 1
                ins.then_inc(s_pch, 1)
                pool.wait_ge(s_pch, steps[0])

            pool.dma_start(con[:, :], const_d).then_inc(s_con, 16)
            pool.dma_start(row[:, :], AP(row_d.tensor, 0, [[0, P], [1, NROW]])).then_inc(s_con, 16)
            pool.dma_start(prf[:, 0:NL * P], mask_d).then_inc(s_con, 16)
            pool.dma_start(poolw[:, :, :], pw_d).then_inc(s_con, 16)
            nc.gpsimd.memset(gs[:, :, :], 0.0).then_inc(s_eps, 1)
            nc.gpsimd.memset(eps[:, :], EPS).then_inc(s_eps, 1)

            def norm(n):
                for c in range(DC):
                    if n == 0:
                        pool.wait_ge(s_x0, 16)
                    else:
                        pool.wait_ge(s_xo, DC * (n - 1) + c + 1)
                    xc = x[:, c * SEQ:(c + 1) * SEQ]
                    if c == 0:
                        link(nc.gpsimd.tensor_tensor(acc[:, :], xc, xc, ALU.mult))
                    else:
                        link(nc.gpsimd.tensor_tensor(sq[:, 0:SEQ], xc, xc, ALU.mult))
                        ins = nc.gpsimd.tensor_tensor(acc[:, :], acc[:, :], sq[:, 0:SEQ], ALU.add)
                        if c < DC - 1:
                            link(ins)
                        else:
                            ins.then_inc(s_acc, 1)

            def square(m, n, g, group):
                c, gains, _ = group
                w = len(gains) * SEQ
                pool.wait_ge(s_y, Y0[n] + c + len(gains))
                if g >= 1:
                    pool.wait_ge(m["qk_normed"], g)
                nc.gpsimd.tensor_tensor(sq[:, 0:w], yc(c, len(gains)), yc(c, len(gains)), ALU.mult).then_inc(m["qk_squared"], 1)

            def key_level(m, b):
                w = LEVELS[b]
                src, dst, nblk = tt[b % 2], tt[(b + 1) % 2], SEQ // w
                step = src.shape[-1]
                pool.wait_ge(m["k_packed"], b + 1)
                if b == 0:
                    pool.wait_ge(m["gates_ready"], 1)
                    pool.wait_ge(m["level_scores"], 1)
                if b >= 1:
                    pool.wait_ge(m["totals"], b)
                for hp in range(2):
                    kv = view(kk[:, hp, 0, 0:1], [[2 * w, nblk // 2], [SEQ + w, 2], [1, w]])
                    tot = view(src[:, 3 * hp + 1, 1:2], [[2, nblk // 2], [step - 1, 2], [0, w]])
                    ins = nc.gpsimd.tensor_tensor(kv, kv, tot, ALU.mult)
                ins.then_inc(m["k_up"], 1)
                if b < NL - 1:
                    if b >= 1:
                        pool.wait_ge(m["q_up"], b)
                    pool.wait_ge(m["k_up"], b + 1)
                    nc.gpsimd.tensor_tensor(view(dst[:, 0, 0:1], [[dst.shape[-1], 6], [1, nblk // 2]]),
                                            view(src[:, 0, 0:1], [[step, 6], [2, nblk // 2]]),
                                            view(src[:, 0, 1:2], [[step, 6], [2, nblk // 2]]),
                                            ALU.mult).then_inc(m["totals"], 1)

            def pool_chunk(m, c, n):
                bufs = (qqf, kkf)
                pool.wait_ge(s_y, Y0[n] + 13 + c)
                if c == 0:
                    nc.gpsimd.memset(qqf[:, 0:8], 0.0)
                    nc.gpsimd.memset(kkf[:, 0:8], 0.0)
                link(nc.gpsimd.tensor_copy(qqf[:, 8:8 + SEQ], yc(12 + c)))
                for k in range(c + 1):
                    a, b = bufs[k % 2], bufs[(k + 1) % 2]
                    link(nc.gpsimd.tensor_tensor(b[:, 8:8 + SEQ], a[:, 8:8 + SEQ], a[:, 8 - 2 ** k:8 - 2 ** k + SEQ], ALU.add))
                p, sums = atf[:, c * SEQ:(c + 1) * SEQ], bufs[(c + 1) % 2]
                nc.gpsimd.tensor_tensor(p[:, 0:16], sums[:, 8:24], con[:, C_INV + 16 * c:C_INV + 16 * (c + 1)], ALU.mult)
                inv = con[:, C_INV + 16 * c + 15:C_INV + 16 * c + 16]
                link(nc.gpsimd.tensor_tensor(p[:, 16:SEQ], sums[:, 24:8 + SEQ], view(inv, [[0, SEQ - 16]]), ALU.mult))
                nc.gpsimd.tensor_tensor(p, p, yc(12 + c), ALU.subtract).then_inc(m["pooled"], 1)

            for n, (kind, l) in enumerate(PHASES):
                norm(n)
                if is_mix[n]:
                    for _, what, g in W[kind]:
                        if what == "sqr":
                            square(M[n], n, g, qk_groups(kind, l)[g])
                        elif what == "level" and g < NL:
                            key_level(M[n], g)
                        elif what == "pool":
                            pool_chunk(M[n], g, n)
                else:
                    F, G = F0[n], G0[n]
                    pool.wait_ge(s_rs, n + 1)
                    with pool.Fori(0, FC // 2) as it:
                        for j in range(2):
                            if kind == "ffn1":
                                pool.wait_ge(s_gelu, it * 2 + (G + j + 1))
                            else:
                                pool.wait_ge(s_tap, it * 2 + (F + j + 1))
                            nc.gpsimd.tensor_tensor(tap[:, j, :], tap[:, j, :], rstd[:, :], ALU.mult).then_inc(s_up, 1)
                            part = ds(it * (2 * SEQ) + j * SEQ, SEQ)
                            pool.wait_ge(s_guh, it * 2 + (F + j + 1))
                            nc.gpsimd.tensor_tensor(gul[:, part], gu[:, j, :], guh[:, part].bitcast(f32),
                                                    ALU.subtract).then_inc(s_gul, 1)

        @block.scalar
        def _(act):
            def split(i, slot, nt, loaded):
                act.wait_ge(s_raw[slot], loaded)
                if not isinstance(i, int) or i >= RING:
                    act.wait_ge(s_pe, i - (RING - 1))
                nc.scalar.activation(wh[:, slot, 0:nt * P], raw[:, slot, 0:nt * P], ACT.Copy).then_inc(s_hi, 1)

            def split_next(i):
                if i < NU:
                    split(i, i % RING, k_tiles(i), 16 * (i // RING + 1))

            def gain_hi(n, c):
                if n < NPH:
                    if n:
                        act.wait_ge(s_xo, c + (DC * (n - 1) + 1))
                    gain, g0 = norm_gain(n)
                    g = PRM[gain] + g0
                    if isinstance(c, int):
                        part, at0 = slice(c * SEQ, (c + 1) * SEQ), slice(g + c, g + c + 1)
                    else:
                        part, at0 = ds(c * SEQ, SEQ), ds(c + g, 1)
                    nc.scalar.activation(hh[:, part], x[:, part], ACT.Copy, scale=prm[:, at0]).then_inc(s_hh, 1)

            def norm(n):
                act.wait_ge(s_ss, n + 1)
                nc.scalar.activation(rstd[:, :], MISC[:, 0:SEQ], ACT.Sqrt, bias=eps[:, 0:1], scale=1.0 / D).then_inc(s_sd, 1)

            def softmax_exp(m, hs, t):
                h = hs[t]
                for k in range(len(h.rows)):
                    r = row0(hs, t) + k
                    if r >= 6:
                        act.wait_ge(m["probs_turned"], row_owner(hs, r - 6) + 1)
                    act.wait_ge(m["maxima"], r + 1)
                    for qt in range(2):
                        cs = slice(qt * SEQ, (qt + 1) * SEQ)
                        o = 2 * (r % 4) + qt
                        src = mb[r % 2][:, cs] if h.bias is None else pr[:, r % 6, cs]
                        acc_out = None if h.cnt is not None else small[:, 8 + o:9 + o]
                        ins = nc.scalar.activation(pr[:, r % 6, cs], src, ACT.Exp, bias=small[:, o:o + 1], scale=h.d ** -0.5,
                                                   accum_out=acc_out)
                    if h.sink is not None:
                        for qt in range(2):
                            o = 2 * (r % 4) + qt
                            ins = nc.scalar.activation(small[:, 24 + o:25 + o], row[:, ROW_SINK + h.sink:ROW_SINK + h.sink + 1],
                                                       ACT.Exp, bias=small[:, o:o + 1])
                    ins.then_inc(m["exps"], 1)

            def pack_keys(m, v):
                w = LEVELS[v - 1]
                if v == 1:
                    act.wait_ge(m["gates_ready"], 1)
                else:
                    act.wait_ge(m["k_up"], v - 1)
                if v >= 3:
                    act.wait_ge(m["level_scores"], v - 1)
                for hp in range(2):
                    ins = nc.scalar.activation(kc[v % 2][:, hp, :].rearrange("p (a b c) -> p a b c", b=2, c=w),
                                               view(kk[:, hp, 0, 0:1], [[2 * w, SEQ // (2 * w)], [SEQ + w, 2], [1, w]]),
                                               ACT.Copy)
                ins.then_inc(m["k_packed"], 1)

            def attention(m, kind, hs, t):
                if 3 <= t < len(hs) + 3:
                    j = t - 3
                    act.wait_ge(m["probs_turned"], j + 1)
                    if j >= 2:
                        act.wait_ge(m["attn_out"], j - 1)
                    nc.scalar.activation(ptb[:, j % 2, :], mb[2][:, :], ACT.Copy).then_inc(m["probsT"], 1)
                if t < len(hs):
                    softmax_exp(m, hs, t)
                if 4 <= t < len(hs) + 4:
                    j = t - 4
                    h = hs[j]
                    if h.chunk is None:
                        act.wait_ge(m["attn_out"], j + 1)
                        nc.scalar.activation(tmo[:, :, 96 * h.h:96 * (h.h + 1)], pair(mb[3][:, :])[:, :, 0:96],
                                             ACT.Copy).then_inc(m["attn_copied"], 1)
                    elif j % 2 == 1:
                        act.wait_ge(m["attn_out"], j + 1)
                        half = (j // 2) % 2
                        nc.scalar.activation(mc(mh, h.chunk), mb[3][:, half * SEQ:(half + 1) * SEQ],
                                             ACT.Copy).then_inc(m["mix_hi"], 1)

            def do(what, g, m, n, kind, l):
                if what == "sum":
                    _, gains, d = qk_groups(kind, l)[g]
                    w = len(gains) * SEQ
                    act.wait_ge(m["qk_sums"], g + 1)
                    nc.scalar.activation(sq[:, 0:w], MISC[:, 0:w], ACT.Sqrt, bias=eps[:, 0:1], scale=1.0 / d).then_inc(m["qk_sd"], 1)
                elif what == "turn":
                    _, w, at0 = V_GROUPS[kind][g]
                    act.wait_ge(m["v_transposed"], g + 1)
                    nc.scalar.activation(tv[:, :, at0:at0 + w * P], pair(MISC[:, :])[:, :, 0:w * P], ACT.Copy).then_inc(m["v_tokens"], 1)
                elif what == "attn":
                    attention(m, kind, heads(kind), g)
                elif what == "gates":
                    act.wait_ge(s_y, Y0[n] + M1_CG + 2)
                    nc.scalar.activation(atf[:, 0:8 * SEQ], yc(M1_CQ, 8), ACT.Sigmoid).then_inc(m["gate_sigs"], 1)
                elif what == "level":
                    if g == 0:
                        pack_keys(m, 1)
                        act.wait_ge(m["level_scores"], 1)
                        for b in range(2):
                            nc.scalar.activation(square_blocks(b), level_bank(gb[2 + b]), ACT.Copy).then_inc(m["diag_copied"], 1)
                    elif g < NL:
                        pack_keys(m, g + 1)
                    elif g == NL + 1:
                        act.wait_ge(m["level_scores"], NL + 2)
                        for b in range(2):
                            nc.scalar.activation(cross_blocks(b), level_bank(gb[2 + b]), ACT.Copy).then_inc(m["diag_copied"], 1)
                elif what == "cout":
                    act.wait_ge(m["mix_psum"], 1)
                    nc.scalar.activation(tmo[:, :, 384:640], pair(gb[2][:, :]), ACT.Copy).then_inc(m["c_copied"], 1)
                elif what == "post":
                    act.wait_ge(m["stats"], 1)
                    nc.scalar.activation(small[:, 64:80], small[:, 48:64], ACT.Sqrt, bias=eps[:, 0:1]).then_inc(m["stats_sd"], 1)
                    for k, (c, w) in enumerate([(3, 2), (5, 2), (7, 1)]):
                        act.wait_ge(m["mix_psum"], k + 2)
                        nc.scalar.activation(mc(mh, c, w), gb[(0, 1, 3)[k]][:, 0:w * SEQ], ACT.Copy).then_inc(m["mix_hi"], 1)
                elif what == "sig":
                    act.wait_ge(s_y, Y0[n] + 2 * g + 2)
                    nc.scalar.activation(yc(2 * g + 1), yc(2 * g + 1), ACT.Sigmoid).then_inc(m["sigmoids"], 1)
                elif what == "ln":
                    act.wait_ge(m["ln_sum"], 2)
                    nc.scalar.activation(rstd[:, :], MISC[:, 0:SEQ], ACT.Sqrt, bias=eps[:, 0:1], scale=1.0 / 512).then_inc(m["ln_sd"], 1)
                    act.wait_ge(m["ln_out"], 1)
                    nc.scalar.activation(every_other(1), every_other(0), ACT.Sigmoid).then_inc(m["ln_sig"], 1)
                    for c in range(4):
                        act.wait_ge(m["mix_sbuf"], c + 1)
                        nc.scalar.activation(mc(mh, c), yc(2 * c), ACT.Copy).then_inc(m["mix_hi"], 1)
                elif what == "pool":
                    act.wait_ge(m["mix_psum"], g + 1)
                    nc.scalar.activation(mc(mh, 4 + g), MISC[:, 0:SEQ], ACT.Copy, scale=col("ps", g)).then_inc(m["mix_hi"], 1)

            def mixer(n, kind, l):
                m, nin = M[n], IN_UNITS[kind]
                for u in range(nin + 1):
                    if u < nin:
                        split_next(U0[n] + u + RING)
                    for what, g in plan(kind, u):
                        do(what, g, m, n, kind, l)
                for o in range(DC):
                    split_next(U0[n] + nin + o + RING)
                    gain_hi(n + 1, o)

            def feed_forward(n, kind, l):
                F, C, U, conv = F0[n], G0[n], U0[n], kind == "ffn1"

                def up(it, j, last):
                    p, i = it * 2 + (F + j), it * 4 + (U + 2 * j)

                    def ahead(k):
                        if last:
                            split_next(i + k + RING)
                        else:
                            b = U + 2 * j + k + RING
                            split(it * 4 + b, b % RING, DC, it * 16 + 16 * (b // RING + 1))

                    if not isinstance(p, int) or p >= 2:
                        act.wait_ge(s_gu, p - 1)
                    act.wait_ge(s_gs, p + 1)
                    gate = gs[:, j, 1:SEQ + 1]
                    if conv:
                        nc.scalar.activation(tap[:, j, :], gate, ACT.Identity,
                                             bias=prm[:, ds(it * 2 + (PRM["cb"] + l * FC + j), 1)],
                                             scale=prm[:, ds(it * 2 + (PRM["cw"] + (3 * l + 1) * FC + j), 1)]).then_inc(s_tap, 1)
                    else:
                        nc.scalar.activation(tap[:, j, :], gate, ACT.Silu).then_inc(s_tap, 1)
                    ahead(0)
                    if conv:
                        act.wait_ge(s_conv, it * 2 + (C + j + 1))
                        nc.scalar.activation(tap[:, j, :], tap[:, j, :], ACT.Gelu).then_inc(s_gelu, 1)
                    ahead(1)
                    act.wait_ge(s_gu, p + 1)
                    nc.scalar.activation(guh[:, ds(it * (2 * SEQ) + j * SEQ, SEQ)], gu[:, j, :], ACT.Copy).then_inc(s_guh, 1)

                for j in range(2):
                    up(0, j, False)
                with act.Fori(1, FC // 2 - 1) as it:
                    for j in range(2):
                        up(it, j, False)
                for j in range(2):
                    up(FC // 2 - 1, j, True)

                def down(it, j, last):
                    b = U + 2 * FC + 2 * j + RING
                    for k in range(2):
                        if last:
                            split_next(it * 4 + b + k)
                            if k == 0:
                                gain_hi(n + 1, it * 2 + j)
                        else:
                            split(it * 4 + (b + k), (b + k) % RING, KD, it * 16 + 16 * ((b + k) // RING + 1))
                            if k == 0:
                                gain_hi(n + 1, it * 2 + j)

                for j in range(2):
                    down(0, j, False)
                with act.Fori(1, 3) as it:
                    for j in range(2):
                        down(it, j, False)
                for j in range(2):
                    down(3, j, True)

            act.wait_ge(s_x0, 16)
            act.wait_ge(s_prm, 16)
            for c in range(DC):
                gain_hi(0, c)
            for i in range(RING):
                split_next(i)
            act.wait_ge(s_ini, 1)
            nc.scalar.activation(par[:, 8:16], par[:, 0:8], ACT.Exp).then_inc(s_inie, 1)
            act.wait_ge(s_eps, 2)
            for n, (kind, l) in enumerate(PHASES):
                norm(n)
                if is_mix[n]:
                    mixer(n, kind, l)
                else:
                    feed_forward(n, kind, l)

        @block.vector
        def _(dve):
            steps = [0]

            def link(ins):
                steps[0] += 1
                ins.then_inc(s_dch, 1)
                dve.wait_ge(s_dch, steps[0])

            def link_second(ins):
                steps[0] += 1
                ins.then_inc(s_dch, 1)
                dve.wait_ge(s_dch, steps[0] - 1)

            def split(i, slot, nt):
                dve.wait_ge(s_hi, i + 1)
                nc.vector.tensor_tensor(wl[:, slot, 0:nt * P], raw[:, slot, 0:nt * P], wh[:, slot, 0:nt * P].bitcast(f32),
                                        ALU.subtract).then_inc(s_lo, 1)

            def split_next(i):
                if i < NU:
                    split(i, i % RING, k_tiles(i))

            def gain_lo(n, c):
                if n < NPH:
                    dve.wait_ge(s_hh, c + (DC * n + 1))
                    gain, g0 = norm_gain(n)
                    g = PRM[gain] + g0
                    if isinstance(c, int):
                        part, at0 = slice(c * SEQ, (c + 1) * SEQ), slice(g + c, g + c + 1)
                    else:
                        part, at0 = ds(c * SEQ, SEQ), ds(c + g, 1)
                    nc.vector.scalar_tensor_tensor(out=hl[:, part], in0=x[:, part], scalar=prm[:, at0],
                                                   in1=hh[:, part].bitcast(f32), op0=ALU.mult, op1=ALU.subtract).then_inc(s_hl, 1)

            def start_values():
                dve.wait_ge(s_prm, 16)
                dve.wait_ge(s_con, 64)
                nc.vector.tensor_copy(msk[:, :, :].rearrange("p a b -> p (a b)"), prf[:, 0:NL * P])
                l0, l1 = prm[:, PRM["lb"]:PRM["lb"] + 2], prm[:, PRM["lb"] + 2:PRM["lb"] + 4]
                link(nc.vector.tensor_tensor(par[:, 16:18], l0, l1, ALU.max))
                nc.vector.tensor_tensor(par[:, 0:2], l0, par[:, 16:18], ALU.subtract)
                nc.vector.tensor_tensor(par[:, 2:4], l1, par[:, 16:18], ALU.subtract)
                prod = qqf[:, 0:192].rearrange("p (a b) -> p a b", a=4)
                link(nc.vector.tensor_tensor(prod, view(row[:, 0:1], [[96, 4], [1, 48]]),
                                             view(row[:, 48:49], [[96, 4], [1, 48]]), ALU.mult))
                nc.vector.reduce_sum(par[:, 4:8], prod, axis=AX.X).then_inc(s_ini, 1)
                dve.wait_ge(s_inie, 1)
                link(nc.vector.tensor_tensor(par[:, 16:18], par[:, 8:10], par[:, 10:12], ALU.add))
                link(nc.vector.reciprocal(par[:, 18:20], par[:, 16:18]))
                nc.vector.tensor_tensor(par[:, 0:2], par[:, 8:10], par[:, 18:20], ALU.mult)
                link(nc.vector.tensor_tensor(par[:, 2:4], par[:, 10:12], par[:, 18:20], ALU.mult))
                link(nc.vector.tensor_tensor(par[:, 4:6], par[:, 0:2], par[:, 2:4], ALU.add))
                link(nc.vector.tensor_tensor(par[:, 20:22], par[:, 0:2], par[:, 0:2], ALU.subtract))
                link(nc.vector.tensor_tensor(par[:, 22:24], par[:, 4:6], par[:, 0:2], ALU.subtract))
                link(nc.vector.tensor_scalar(par[:, 20:24], par[:, 20:24], 0.0, None, ALU.max))
                link(nc.vector.tensor_scalar(par[:, 24:28], par[:, 20:24], -1.0, 1.0, ALU.mult, ALU.add))
                for l in range(2):
                    lam0 = 0.8 - 0.6 * math.exp(-0.3 * l)
                    link(nc.vector.tensor_tensor(par[:, 28 + l:29 + l], par[:, 13 + 2 * l:14 + 2 * l],
                                                 par[:, 12 + 2 * l:13 + 2 * l], ALU.subtract))
                    link(nc.vector.tensor_scalar(par[:, 28 + l:29 + l], par[:, 28 + l:29 + l], lam0, None, ALU.subtract))

            def norm(n):
                dve.wait_ge(s_sd, n + 1)
                nc.vector.reciprocal(rstd[:, :], rstd[:, :]).then_inc(s_rs, 1)
                dve.wait_ge(s_rs, n + 1)

            def head_norm(m, g, kind, l):
                c, gains, _ = qk_groups(kind, l)[g]
                dve.wait_ge(m["qk_sd"], g + 1)
                w = len(gains) * SEQ
                link(nc.vector.reciprocal(sq[:, 0:w], sq[:, 0:w]))
                for k, (name, at0) in enumerate(gains):
                    ins = nc.vector.scalar_tensor_tensor(out=yc(c + k), in0=yc(c + k), scalar=col(name, at0),
                                                         in1=sq[:, k * SEQ:(k + 1) * SEQ], op0=ALU.mult, op1=ALU.mult)
                ins.then_inc(m["qk_normed"], 1)

            def rope(m, g):
                def both(at0):
                    return view(con[:, at0:at0 + 1], [[0, 2], [1, SEQ]])
                yv, tmp = pair(yc(2 * g, 2)), pair(ptb[:, 0, :])
                dve.wait_ge(m["rotated"], g + 1)
                nc.vector.tensor_tensor(tmp, pair(MISC[:, :]), both(C_SIN), ALU.mult)
                link(nc.vector.tensor_tensor(yv, yv, both(C_COS), ALU.mult))
                nc.vector.tensor_tensor(yv, yv, tmp, ALU.add).then_inc(m["roped"], 1)

            def gates(m, l):
                e = atf[:, 0:8 * SEQ]
                dve.wait_ge(m["gate_sigs"], 1)
                nc.vector.tensor_tensor(yc(M1_CQ, 2), yc(M1_CQ, 2), e[:, 0:2 * SEQ], ALU.mult)
                nc.vector.tensor_tensor(yc(M1_CG, 2), yc(M1_CG, 2), e[:, 6 * SEQ:8 * SEQ], ALU.mult)
                t0 = tt[0]
                for hp in range(2):
                    lb, rest = par[:, 20 + 2 * l + hp:21 + 2 * l + hp], par[:, 24 + 2 * l + hp:25 + 2 * l + hp]
                    for slot, src in ((0, 4 + hp), (1, 2 + hp), (2, 4 + hp)):
                        last = nc.vector.tensor_scalar(t0[:, 3 * hp + slot, :], e[:, src * SEQ:(src + 1) * SEQ], rest, lb,
                                                       ALU.mult, ALU.add)
                link(last)
                link(nc.vector.tensor_scalar(t0[:, :, :], t0[:, :, :], 1e-20, None, ALU.max))
                for hp in range(2):
                    nc.vector.tensor_scalar(kk[:, hp, :, :], t0[:, 3 * hp + 1:3 * hp + 3, :], -1.0, 1.0, ALU.mult, ALU.add)
                    last = nc.vector.tensor_tensor(qq[:, hp, :, :], t0[:, 3 * hp:3 * hp + 2, :],
                                                   view(yc(M1_CQ + hp)[:, 0:1], [[0, 2], [1, SEQ]]), ALU.mult)
                last.then_inc(m["gates_ready"], 1)

            def convolve(m, c, part):
                taps = PRM["ecw"] + 31 * c
                val, gate = yc(2 * c), yc(2 * c + 1)
                if part == 0:
                    dve.wait_ge(m["sigmoids"], c + 1)
                    if c == 0:
                        nc.vector.memset(qqf[:, 0:30], 0.0)
                    link(nc.vector.tensor_tensor(qqf[:, 30:30 + SEQ], val, gate, ALU.mult))
                    nc.vector.tensor_scalar(val, qqf[:, 0:SEQ], prm[:, taps:taps + 1], col("ecb", c), ALU.mult, ALU.add)
                    link(nc.vector.tensor_scalar(gate, qqf[:, 1:1 + SEQ], prm[:, taps + 1:taps + 2], None, ALU.mult))
                for k in range(max(2, 8 * part), min(31, 8 * part + 8)):
                    s = (val, gate)[k % 2]
                    link_second(nc.vector.scalar_tensor_tensor(out=s, in0=qqf[:, k:k + SEQ], scalar=prm[:, taps + k:taps + k + 1],
                                                               in1=s, op0=ALU.mult, op1=ALU.add))
                dve.wait_ge(s_dch, steps[0])
                if part == 3:
                    link(nc.vector.tensor_tensor(val, val, gate, ALU.add))

            def layer_norm(m):
                link(nc.vector.tensor_tensor(acc[:, :], yc(0), yc(2), ALU.add))
                link(nc.vector.tensor_tensor(acc[:, :], acc[:, :], yc(4), ALU.add))
                nc.vector.tensor_tensor(acc[:, :], acc[:, :], yc(6), ALU.add).then_inc(m["ln_operand"], 1)
                dve.wait_ge(m["ln_sum"], 1)
                for c in range(4):
                    last = nc.vector.scalar_tensor_tensor(out=yc(2 * c), in0=MISC[:, 0:SEQ], scalar=-1.0 / 512,
                                                          in1=yc(2 * c), op0=ALU.mult, op1=ALU.add)
                link(last)
                link(nc.vector.tensor_tensor(every_other(1), every_other(0), every_other(0), ALU.mult))
                nc.vector.tensor_tensor(yc(1), yc(1), yc(5), ALU.add)
                link(nc.vector.tensor_tensor(yc(3), yc(3), yc(7), ALU.add))
                nc.vector.tensor_tensor(acc[:, :], yc(1), yc(3), ALU.add).then_inc(m["ln_operand"], 1)
                dve.wait_ge(m["ln_sd"], 1)
                link(nc.vector.reciprocal(rstd[:, :], rstd[:, :]))
                for c in range(4):
                    last = nc.vector.scalar_tensor_tensor(out=yc(2 * c), in0=yc(2 * c), scalar=col("lng", c), in1=rstd[:, :],
                                                          op0=ALU.mult, op1=ALU.mult)
                link(last)
                for c in range(4):
                    last = nc.vector.tensor_scalar(yc(2 * c), yc(2 * c), col("lnb", c), None, ALU.add)
                last.then_inc(m["ln_out"], 1)
                dve.wait_ge(m["ln_sig"], 1)
                for c in range(4):
                    nc.vector.tensor_tensor(yc(2 * c), yc(2 * c), yc(2 * c + 1), ALU.mult).then_inc(m["mix_sbuf"], 1)
                done = before("even", "ln", 0)
                for c in range(4):
                    dve.wait_ge(m["mix_hi"], done + c + 1)
                    nc.vector.tensor_tensor(mc(ml, c), yc(2 * c), mc(mh, c).bitcast(f32), ALU.subtract).then_inc(m["mix_lo"], 1)

            def row_max(m, hs, t):
                h = hs[t]
                for k in range(len(h.rows)):
                    r = row0(hs, t) + k
                    o = 2 * (r % 4)
                    dve.wait_ge(m["scores"], r + 1)
                    s, scale = mb[r % 2][:, :], h.d ** -0.5
                    if h.bias is not None:
                        if r >= 6:
                            dve.wait_ge(m["probs_turned"], row_owner(hs, r - 6) + 1)
                        link(nc.vector.scalar_tensor_tensor(out=pr[:, r % 6, :], in0=tab[:, 0:512], scalar=h.bias,
                                                            in1=s, op0=ALU.mult, op1=ALU.add))
                        s = pr[:, r % 6, :]
                    link(nc.vector.reduce_max(small[:, 16 + o:18 + o], pair(s), axis=AX.X))
                    if h.sink is not None:
                        link(nc.vector.tensor_scalar(small[:, 16 + o:18 + o], small[:, 16 + o:18 + o], scale,
                                                     row[:, ROW_SINK + h.sink:ROW_SINK + h.sink + 1], ALU.mult, ALU.max))
                        scale = 1.0
                    nc.vector.tensor_scalar(small[:, o:o + 2], small[:, 16 + o:18 + o], -scale, None, ALU.mult).then_inc(m["maxima"], 1)

            def normalise(m, hs, t, l):
                h = hs[t]
                r, nr = row0(hs, t), len(h.rows)
                o = 2 * (r % 4)
                sums = small[:, 8 + o:8 + o + 2 * nr]
                dve.wait_ge(m["exps"], r + nr)
                if h.cnt is not None:
                    link(nc.vector.tensor_tensor(pr[:, r % 6, :], pr[:, r % 6, :], tab[:, 512:1024], ALU.mult))
                    link(nc.vector.reduce_sum(sums, pair(pr[:, r % 6, :]), axis=AX.X))
                if h.sink is not None:
                    link(nc.vector.tensor_tensor(sums, sums, small[:, 24 + o:26 + o], ALU.add))
                link(nc.vector.reciprocal(small[:, 80 + o:80 + o + 2 * nr], sums))
                if nr == 2:
                    link(nc.vector.tensor_scalar(small[:, 82 + o:84 + o], small[:, 82 + o:84 + o], par[:, 28 + l:29 + l], None, ALU.mult))
                    for qt in range(2):
                        p2 = pr[:, (r + 1) % 6, qt * SEQ:(qt + 1) * SEQ]
                        last = nc.vector.tensor_scalar(p2, p2, small[:, 82 + o + qt:83 + o + qt], None, ALU.mult)
                    link(last)
                for qt in range(2):
                    p1 = pr[:, r % 6, qt * SEQ:(qt + 1) * SEQ]
                    if nr == 2:
                        last = nc.vector.scalar_tensor_tensor(out=p1, in0=p1, scalar=small[:, 80 + o + qt:81 + o + qt],
                                                              in1=pr[:, (r + 1) % 6, qt * SEQ:(qt + 1) * SEQ], op0=ALU.mult, op1=ALU.add)
                    else:
                        last = nc.vector.tensor_scalar(p1, p1, small[:, 80 + o + qt:81 + o + qt], None, ALU.mult)
                last.then_inc(m["probs"], 1)

            def level(m, v):
                b = v - 1
                w, src, nblk = LEVELS[b], tt[b % 2], SEQ // LEVELS[b]
                dve.wait_ge(m["level_scores"], v + 1)
                if v == 1:
                    dve.wait_ge(m["diag_copied"], 2)
                for k in range(2):
                    nc.vector.copy_predicated(square_blocks(k), view(msk[:, b, 0:1], [[0, 2], [0, 2], [1, P]]),
                                              level_bank(gb[2 + k])).then_inc(m["level_copied"], 1)
                if b >= 1:
                    dve.wait_ge(m["totals"], b)
                for hp in range(2):
                    qv = view(qq[:, hp, 0, 0:1], [[2 * w, nblk // 2], [SEQ + w, 2], [1, w]])
                    tot = view(src[:, 3 * hp, 1:2], [[2, nblk // 2], [src.shape[-1] - 1, 2], [0, w]])
                    ins = nc.vector.tensor_tensor(qv, qv, tot, ALU.mult)
                ins.then_inc(m["q_up"], 1)

            def attention(m, kind, hs, t, l):
                if t < len(hs):
                    row_max(m, hs, t)
                if 1 <= t <= len(hs):
                    normalise(m, hs, t - 1, l)
                if outputs(kind, "attn", t):
                    j = (t - 4) // 2
                    c = hs[t - 4].chunk
                    dve.wait_ge(m["mix_hi"], before(kind, "attn", t) + 1)
                    nc.vector.tensor_tensor(mc(ml, c), mb[3][:, (j % 2) * SEQ:(j % 2 + 1) * SEQ],
                                            mc(mh, c).bitcast(f32), ALU.subtract).then_inc(m["mix_lo"], 1)

            def out_norms(m, l):
                dve.wait_ge(m["c_copied"], 1)
                dve.wait_ge(m["attn_copied"], 4)
                link(nc.vector.tensor_tensor(tms, tmo, tmo, ALU.mult))
                rb = small[:, 48:56].rearrange("p (a b) -> p a b", a=2)
                rc = small[:, 56:64].rearrange("p (a b) -> p a b", a=2)
                for tile in range(2):
                    nc.vector.reduce_sum(rb[:, tile, :], tms[:, tile, 0:384].rearrange("p (h d) -> p h d", h=4), axis=AX.X)
                    last = nc.vector.reduce_sum(rc[:, tile, :], tms[:, tile, 384:640].rearrange("p (h d) -> p h d", h=4), axis=AX.X)
                link(last)
                nc.vector.tensor_scalar(small[:, 48:56], small[:, 48:56], 1.0 / 96, None, ALU.mult)
                nc.vector.tensor_scalar(small[:, 56:64], small[:, 56:64], 1.0 / 64, None, ALU.mult).then_inc(m["stats"], 1)
                dve.wait_ge(m["stats_sd"], 1)
                link(nc.vector.reciprocal(small[:, 64:80], small[:, 64:80]))
                keep = 1.0 - (0.8 - 0.6 * math.exp(-0.3 * l))
                for tile in range(2):
                    for part, w, s0 in ((tmo[:, tile, 0:384], 96, 64 + 4 * tile), (tmo[:, tile, 384:640], 64, 72 + 4 * tile)):
                        pv = part.rearrange("p (h d) -> p h d", h=4)
                        last = nc.vector.tensor_tensor(pv, pv, view(small[:, s0:s0 + 1], [[1, 4], [0, w]]), ALU.mult)
                link(last)
                for tile in range(2):
                    b, c = tmo[:, tile, 0:384], tmo[:, tile, 384:640]
                    nc.vector.scalar_tensor_tensor(out=b, in0=b, scalar=keep, in1=row[:, ROW_SUB + 384 * l:ROW_SUB + 384 * (l + 1)],
                                                   op0=ALU.mult, op1=ALU.mult)
                    last = nc.vector.tensor_tensor(c, c, row[:, ROW_CON + 256 * l:ROW_CON + 256 * (l + 1)], ALU.mult)
                link(last)
                nc.vector.tensor_tensor(tmo[:, :, 384:640], tmo[:, :, 384:640], tv[:, :, 768:1024], ALU.mult).then_inc(m["mix_sbuf"], 1)
                done = before("mix1", "post", 0)
                for g, (c, w) in enumerate([(3, 2), (5, 2), (7, 1)]):
                    dve.wait_ge(m["mix_hi"], done + g + 1)
                    nc.vector.tensor_tensor(mc(ml, c, w), gb[(0, 1, 3)[g]][:, 0:w * SEQ],
                                            mc(mh, c, w).bitcast(f32), ALU.subtract).then_inc(m["mix_lo"], 1)

            def do(what, g, m, n, kind, l):
                if what == "norm":
                    head_norm(m, g, kind, l)
                elif what == "rope":
                    rope(m, g)
                elif what == "gates":
                    gates(m, l)
                elif what == "conv":
                    convolve(m, g // 4, g % 4)
                elif what == "attn":
                    attention(m, kind, heads(kind), g, l)
                elif what == "level" and 1 <= g <= NL:
                    level(m, g)
                elif what == "post":
                    out_norms(m, l)
                elif what == "ln":
                    layer_norm(m)
                elif what == "pool":
                    dve.wait_ge(m["mix_hi"], before(kind, "pool", g) + 1)
                    nc.vector.scalar_tensor_tensor(out=mc(ml, 4 + g), in0=MISC[:, 0:SEQ], scalar=col("ps", g),
                                                   in1=mc(mh, 4 + g).bitcast(f32), op0=ALU.mult, op1=ALU.subtract).then_inc(m["mix_lo"], 1)

            def mixer(n, kind, l):
                m, nin = M[n], IN_UNITS[kind]
                dve.wait_ge(s_tab, T0[n])
                for u in range(nin + 1):
                    if u < nin:
                        dve.wait_ge(s_pe, U0[n] + u + 1)
                        nc.vector.tensor_tensor(yc(u), gb[bank_of(kind, u)][:, 0:SEQ], rstd[:, :], ALU.mult).then_inc(s_y, 1)
                        split_next(U0[n] + u + RING)
                    for what, g in plan(kind, u):
                        do(what, g, m, n, kind, l)
                for o in range(DC):
                    u = nin + o
                    dve.wait_ge(s_pe, U0[n] + u + 1)
                    xc = x[:, o * SEQ:(o + 1) * SEQ]
                    nc.vector.tensor_tensor(xc, gb[o % 4][:, 0:SEQ], xc, ALU.add).then_inc(s_xo, 1)
                    split_next(U0[n] + u + RING)
                    gain_lo(n + 1, o)

            def feed_forward(n, kind, l):
                F, C, U, conv = F0[n], G0[n], U0[n], kind == "ffn1"

                def up(it, j, last):
                    p, i = it * 2 + (F + j), it * 4 + (U + 2 * j)
                    val, t = gb[2 * j + 1], tap[:, j, :]

                    def ahead(k):
                        if last:
                            split_next(i + k + RING)
                        else:
                            b = U + 2 * j + k + RING
                            split(it * 4 + b, b % RING, DC)

                    dve.wait_ge(s_pe, i + 1)
                    nc.vector.tensor_tensor(gs[:, j, 1:SEQ + 1], gb[2 * j][:, 0:SEQ], rstd[:, :], ALU.mult).then_inc(s_gs, 1)
                    if not conv:
                        ahead(0)
                    else:
                        w0 = prm[:, ds(it * 2 + (PRM["cw"] + 3 * l * FC + j), 1)]
                        w2 = prm[:, ds(it * 2 + (PRM["cw"] + (3 * l + 2) * FC + j), 1)]
                        dve.wait_ge(s_tap, p + 1)
                        nc.vector.scalar_tensor_tensor(out=t, in0=gs[:, j, 0:SEQ], scalar=w0, in1=t,
                                                       op0=ALU.mult, op1=ALU.add).then_inc(s_c1, 1)
                        dve.wait_ge(s_c1, it * 2 + (C + j + 1))
                        nc.vector.scalar_tensor_tensor(out=t, in0=gs[:, j, 2:SEQ + 2], scalar=w2, in1=t,
                                                       op0=ALU.mult, op1=ALU.add).then_inc(s_conv, 1)
                        ahead(0)
                    dve.wait_ge(s_up, p + 1)
                    dve.wait_ge(s_pe, i + 2)
                    if not isinstance(p, int) or p >= 2:
                        dve.wait_ge(s_gul, p - 1)
                    nc.vector.tensor_tensor(gu[:, j, :], val[:, 0:SEQ], t, ALU.mult).then_inc(s_gu, 1)
                    ahead(1)

                def down(it, j, last):
                    b = U + 2 * FC + 2 * j

                    def ahead(k):
                        if last:
                            split_next(it * 4 + b + k + RING)
                        else:
                            split(it * 4 + (b + k + RING), (b + k) % RING, KD)

                    ahead(0)
                    dve.wait_ge(s_pe, it * 4 + (b + 2))
                    xc = x[:, ds(it * (2 * SEQ) + j * SEQ, SEQ)]
                    nc.vector.scalar_tensor_tensor(out=xc, in0=gb[j][:, 0:SEQ], scalar=1.0 if conv else 0.5, in1=xc,
                                                   op0=ALU.mult, op1=ALU.add).then_inc(s_xo, 1)
                    gain_lo(n + 1, it * 2 + j)
                    ahead(1)

                for one, trips in ((up, FC // 2 - 1), (down, 3)):
                    for j in range(2):
                        one(0, j, False)
                    with dve.Fori(1, trips) as it:
                        for j in range(2):
                            one(it, j, False)
                    for j in range(2):
                        one(trips, j, True)

            dve.wait_ge(s_x0, 16)
            dve.wait_ge(s_prm, 16)
            for c in range(DC):
                gain_lo(0, c)
            for i in range(RING):
                split_next(i)
            start_values()
            dve.wait_ge(s_eps, 2)
            for n, (kind, l) in enumerate(PHASES):
                norm(n)
                if is_mix[n]:
                    mixer(n, kind, l)
                else:
                    feed_forward(n, kind, l)

        @block.tensor
        def _(pe):
            def tiles(i, slot, bank, nt, rhs_h, rhs_l, start, stop, ready=None):
                pe.wait_ge(s_lo, i + 1)
                for k in range(nt):
                    if ready is not None:
                        ready(k)
                    a, b = wh[:, slot, k * P:(k + 1) * P], wl[:, slot, k * P:(k + 1) * P]
                    nc.tensor.matmul(bank, a, rhs_h(k), start=start and k == 0, stop=False)
                    nc.tensor.matmul(bank, a, rhs_l(k), start=False, stop=False)
                    last = nc.tensor.matmul(bank, b, rhs_h(k), start=False, stop=stop and k == nt - 1)
                last.then_inc(s_pe, 1)

            def norm(n):
                pe.wait_ge(s_acc, n + 1)
                if n == 0:
                    pe.wait_ge(s_con, 64)
                nc.tensor.matmul(MISC[:, 0:SEQ], ones, acc[:, :], start=True, stop=True).then_inc(s_ss, 1)

            def first_unit(n):
                i = U0[n]
                if n:
                    pe.wait_ge(s_xo, DC * n - 1)
                tiles(i, i % RING, gb[0][:, 0:SEQ], DC, lambda k: mc(hh, k), lambda k: mc(hl, k), True, True,
                      lambda k: pe.wait_ge(s_hl, DC * n + k + 1))
                norm(n)

            reader = [None]

            def take_misc(sem, value):
                if reader[0] is not None:
                    pe.wait_ge(*reader[0])
                reader[0] = (sem, value)

            def level(m, v, n):
                if v == 0:
                    pe.wait_ge(m["gates_ready"], 1)
                    pe.wait_ge(s_y, Y0[n] + 13)
                else:
                    if v >= 2:
                        pe.wait_ge(m["q_up"], v - 1)
                        pe.wait_ge(m["level_copied"], 2 * (v - 1))
                    else:
                        pe.wait_ge(m["diag_copied"], 2)
                    if v <= NL:
                        pe.wait_ge(m["k_packed"], v)
                    else:
                        pe.wait_ge(m["k_up"], NL)
                for i in range(2):
                    for h in range(4):
                        hp, b0 = h // 2, 64 * (h % 2)
                        part = slice(b0, b0 + 64)
                        o = gb[2 + h % 2][:, (2 * hp + i) * P:(2 * hp + i + 1) * P]
                        ts = slice(i * P, (i + 1) * P)
                        if v == 0:
                            q = y[part, (M1_CQ + hp) * SEQ + i * P:(M1_CQ + hp) * SEQ + (i + 1) * P]
                            nc.tensor.matmul(o, kk[part, hp, 0, ts], q, start=True, stop=False)
                            last = nc.tensor.matmul(o, kk[part, hp, 1, ts], q, start=False, stop=True)
                        elif v <= NL:
                            w = LEVELS[v - 1]
                            dims = [[2 * w, P // (2 * w)], [SEQ + w, 2], [1, w]]
                            last = nc.tensor.matmul(o, kc[v % 2][part, hp, ts],
                                                    view(qq[part, hp, 0, i * P:i * P + 1], dims), start=True, stop=True)
                        else:
                            last = nc.tensor.matmul(o, kk[part, hp, i, ts], qq[part, hp, 1 - i, (1 - i) * P:(2 - i) * P],
                                                    start=True, stop=True)
                last.then_inc(m["level_scores"], 1)

            def scores(m, kind, l, hs, t):
                need = max(group_of(kind, l, c) for qc, kc_, _ in hs[t].rows for c in (qc, kc_))
                pe.wait_ge(m["qk_normed"], need + 1)
                if kind == "mix1":
                    pe.wait_ge(m["roped"], 2)
                for k, (qc, kc_, b0) in enumerate(hs[t].rows):
                    r = row0(hs, t) + k
                    part = slice(b0, b0 + hs[t].d)
                    if r >= 2:
                        pe.wait_ge(m["maxima" if BIASED[kind][r - 2] else "exps"], r - 1)
                    for qt in range(2):
                        last = nc.tensor.matmul(mb[r % 2][:, qt * SEQ:(qt + 1) * SEQ],
                                                y[part, qc * SEQ + qt * P:qc * SEQ + (qt + 1) * P],
                                                y[part, kc_ * SEQ:(kc_ + 1) * SEQ], start=True, stop=True)
                    last.then_inc(m["scores"], 1)

            def turn_probs(m, hs, t):
                r = row0(hs, t) % 6
                pe.wait_ge(m["probs"], t + 1)
                take_misc(m["probsT"], t + 1)
                for kt in range(2):
                    for qt in range(2):
                        last = nc.tensor.transpose(mb[2][:, kt * SEQ + qt * P:kt * SEQ + (qt + 1) * P],
                                                   pr[:, r, qt * SEQ + kt * P:qt * SEQ + (kt + 1) * P], ident)
                last.then_inc(m["probs_turned"], 1)

            def attend(m, kind, hs, t):
                h = hs[t]
                groups = V_GROUPS[kind]
                pe.wait_ge(m["v_tokens"], 1 if kind == "mix1" and h.chunk is not None else len(groups))
                pe.wait_ge(m["probsT"], t + 1)
                pt = ptb[:, t % 2, :]
                if h.chunk is None:
                    if h.h == 0:
                        pe.wait_ge(m["mix_lo"], 3)
                    else:
                        pe.wait_ge(m["attn_copied"], h.h)
                    for qt in range(2):
                        for kt in range(2):
                            last = nc.tensor.matmul(mb[3][:, qt * SEQ:qt * SEQ + 96], pt[:, kt * SEQ + qt * P:kt * SEQ + (qt + 1) * P],
                                                    tv[:, kt, h.v:h.v + h.vw], start=kt == 0, stop=kt == 1)
                else:
                    j = t // 2
                    if j >= 1 and t % 2 == 0:
                        pe.wait_ge(m["mix_lo"], before(kind, "attn", 2 * j + 3) + 1)
                    for kt in range(2):
                        last = nc.tensor.matmul(mb[3][h.base:h.base + 64, (j % 2) * SEQ:(j % 2 + 1) * SEQ],
                                                tv[:, kt, h.v:h.v + h.vw], pt[:, kt * SEQ:(kt + 1) * SEQ], start=kt == 0, stop=kt == 1)
                last.then_inc(m["attn_out"], 1)

            def do(what, g, m, n, kind, l):
                if what == "sum":
                    w = len(qk_groups(kind, l)[g][1]) * SEQ
                    pe.wait_ge(m["qk_squared"], g + 1)
                    take_misc(m["qk_sd"], g + 1)
                    nc.tensor.matmul(MISC[:, 0:w], con[:, C_BLK:C_BLK + P], sq[:, 0:w], start=True, stop=True).then_inc(m["qk_sums"], 1)
                elif what == "rotate":
                    pe.wait_ge(m["qk_normed"], g + 1)
                    take_misc(m["roped"], g + 1)
                    nc.tensor.matmul(MISC[:, :], con[:, C_PERM:C_PERM + P], yc(2 * g, 2), start=True, stop=True).then_inc(m["rotated"], 1)
                elif what == "turn":
                    c, w, _ = V_GROUPS[kind][g]
                    if c == M1_CG and kind == "mix1":
                        pe.wait_ge(m["gates_ready"], 1)
                    pe.wait_ge(s_y, Y0[n] + c + w)
                    take_misc(m["v_tokens"], g + 1)
                    for cc in range(w):
                        for tile in range(2):
                            last = nc.tensor.transpose(MISC[:, tile * SEQ + cc * P:tile * SEQ + (cc + 1) * P],
                                                       y[:, (c + cc) * SEQ + tile * P:(c + cc) * SEQ + (tile + 1) * P], ident)
                    last.then_inc(m["v_transposed"], 1)
                elif what == "attn":
                    hs = heads(kind)
                    if 3 <= g < len(hs) + 3:
                        turn_probs(m, hs, g - 3)
                    if g < len(hs):
                        scores(m, kind, l, hs, g)
                    if 4 <= g < len(hs) + 4:
                        attend(m, kind, hs, g - 4)
                elif what == "level":
                    level(m, g, n)
                elif what == "cout":
                    pe.wait_ge(m["diag_copied"], 4)
                    pe.wait_ge(m["level_copied"], 2 * NL)
                    pe.wait_ge(m["v_tokens"], 3)
                    for tile in range(2):
                        for h in range(4):
                            for s in range(2):
                                last = nc.tensor.matmul(gb[2][:, tile * SEQ + 64 * h:tile * SEQ + 64 * (h + 1)],
                                                        at[:, s, h, tile * P:(tile + 1) * P], tv[:, s, 512 + 64 * h:512 + 64 * (h + 1)],
                                                        start=s == 0, stop=s == 1)
                    last.then_inc(m["mix_psum"], 1)
                elif what == "post":
                    pe.wait_ge(m["mix_sbuf"], 1)
                    pe.wait_ge(s_y, Y0[n] + IN_UNITS[kind])
                    for k, (c, w) in enumerate([(3, 2), (5, 2), (7, 1)]):
                        for cc in range(w):
                            for tile in range(2):
                                at0 = (c - 3 + cc) * P
                                last = nc.tensor.transpose(gb[(0, 1, 3)[k]][:, cc * SEQ + tile * P:cc * SEQ + (tile + 1) * P],
                                                           tmo[:, tile, at0:at0 + P], ident)
                        last.then_inc(m["mix_psum"], 1)
                elif what == "ln":
                    pe.wait_ge(m["ln_operand"], 1)
                    take_misc(m["ln_operand"], 2)
                    nc.tensor.matmul(MISC[:, 0:SEQ], ones, acc[:, :], start=True, stop=True).then_inc(m["ln_sum"], 1)
                    take_misc(m["ln_sd"], 1)
                    nc.tensor.matmul(MISC[:, 0:SEQ], ones, acc[:, :], start=True, stop=True).then_inc(m["ln_sum"], 1)
                elif what == "pool":
                    pe.wait_ge(m["pooled"], g + 1)
                    take_misc(m["mix_lo"], before(kind, "pool", g) + 1)
                    nc.tensor.matmul(MISC[:, 0:SEQ], poolw[:, g, :], atf[:, g * SEQ:(g + 1) * SEQ], start=True,
                                     stop=True).then_inc(m["mix_psum"], 1)

            def mixer(n, kind, l):
                m, nin = M[n], IN_UNITS[kind]
                reader[0] = (s_sd, n + 1)
                for u in range(nin + 1):
                    i = U0[n] + u
                    if u == 0:
                        first_unit(n)
                    elif u < nin:
                        if freed_by(kind, u):
                            pe.wait_ge(s_y, Y0[n] + freed_by(kind, u))
                        tiles(i, i % RING, gb[bank_of(kind, u)][:, 0:SEQ], DC, lambda k: mc(hh, k), lambda k: mc(hl, k), True, True)
                    for what, g in plan(kind, u):
                        do(what, g, m, n, kind, l)
                pe.wait_ge(m["mix_lo"], MIX_OUT[kind])
                for o in range(DC):
                    i = U0[n] + nin + o
                    if o >= 4:
                        pe.wait_ge(s_xo, DC * n + o - 3)
                    tiles(i, i % RING, gb[o % 4][:, 0:SEQ], DC, lambda k: mc(mh, k), lambda k: mc(ml, k), True, True)

            def feed_forward(n, kind, l):
                F, U = F0[n], U0[n]

                def up(it, j, first):
                    for k in range(2):
                        i = it * 4 + (U + 2 * j + k)
                        if first and j + k == 0:
                            first_unit(n)
                            continue
                        if not first and k == 0:
                            pe.wait_ge(s_gu, it * 2 + (F + j - 1))
                        tiles(i, (U + 2 * j + k) % RING, gb[2 * j + k][:, 0:SEQ], DC, lambda k: mc(hh, k), lambda k: mc(hl, k),
                              True, True)

                for j in range(2):
                    up(0, j, True)
                with pe.Fori(1, FC // 2) as it:
                    for j in range(2):
                        up(it, j, False)

                def down(it, j, first):
                    for k in range(2):
                        b = U + 2 * FC + 2 * j + k
                        if not first and k == 0:
                            pe.wait_ge(s_xo, it * 2 + (DC * n + j - 1))
                        tiles(it * 4 + b, b % RING, gb[j][:, 0:SEQ], KD,
                              lambda c: guh[:, (k * KD + c) * SEQ:(k * KD + c + 1) * SEQ],
                              lambda c: gul[:, (k * KD + c) * SEQ:(k * KD + c + 1) * SEQ], k == 0, k == 1,
                              (lambda c: pe.wait_ge(s_gul, F + k * KD + c + 1)) if first and j == 0 else None)

                pe.wait_ge(s_gu, F + FC - 1)
                for j in range(2):
                    down(0, j, True)
                with pe.Fori(1, 4) as it:
                    for j in range(2):
                        down(it, j, False)

            for n, (kind, l) in enumerate(PHASES):
                if is_mix[n]:
                    mixer(n, kind, l)
                else:
                    feed_forward(n, kind, l)


def units_of(w):
    k, n = w.shape
    return w.reshape(k // P, P, n // P, P).transpose(2, 1, 0, 3).reshape(n // P, P, k)


def up_units(gate, val):
    g, v = units_of(gate), units_of(val)
    return np.stack([g, v], 1).reshape(2 * g.shape[0], P, -1)


def down_units(w):
    u = units_of(w)
    return u.reshape(DC, P, 2, KD * P).transpose(0, 2, 1, 3).reshape(2 * DC, P, KD * P)


def pad_to(a, n, axis):
    shape = list(a.shape)
    shape[axis] = n - shape[axis]
    return np.concatenate([a, np.zeros(shape, a.dtype)], axis)


def per_chunk(v):
    return v.reshape(-1, P).T


def kernel(**inputs):
    import concourse.bacc as _bacc
    from concourse import mybir as _mybir
    from concourse.bass_utils import run_bass_kernel_spmd as _run

    a = {k: np.asarray(v) for k, v in inputs.items()}
    ff = FC * P

    def m1_columns(w):
        c = np.split(w, np.cumsum([384, 128, 128, 384, 384, 384, 256, 256, 256, 256]), axis=1)
        aq, ak, av, bq, bk, bv, cq, cf, cb, cv, cg = c
        aq = aq.reshape(D, 2, 3, 64).transpose(0, 2, 1, 3).reshape(D, 384)
        bq, bk = (pad_to(t.reshape(D, 8, 48), 64, 2).reshape(D, 512) for t in (bq, bk))
        bqk = np.stack([bq.reshape(D, 4, P), bk.reshape(D, 4, P)], 2).reshape(D, 1024)
        return np.concatenate([aq, ak, av, cq, cf, cb, cg, cv, bv, bqk], 1)

    def m1_rows(w):
        return np.concatenate([w[:384].reshape(2, 3, 64, D).transpose(1, 0, 2, 3).reshape(384, D), w[384:]], 0)

    def ev_columns(w):
        val, gate, q, k, v = np.split(w, np.cumsum([512, 512, 512, 128]), axis=1)
        q = q.reshape(D, 2, 4, 64).transpose(0, 2, 1, 3).reshape(D, 512)
        vg = np.stack([val.reshape(D, 4, P), gate.reshape(D, 4, P)], 2).reshape(D, 1024)
        return np.concatenate([vg, v, k, q], 1)

    def od_columns(w):
        q, k, v, u = np.split(w, 4, axis=1)
        qk = np.stack([q.reshape(D, 4, P), k.reshape(D, 4, P)], 2).reshape(D, 1024)
        return np.concatenate([v, qk, u], 1)

    def ev_rows(w):
        return np.concatenate([w[:512], w[512:].reshape(2, 4, 64, D).transpose(1, 0, 2, 3).reshape(512, D)], 0)

    wa, wb = [], []
    for kind, l in PHASES:
        if kind == "mix1":
            wa += [units_of(m1_columns(a["w_in"][l])), units_of(m1_rows(a["w_out"][l]))]
        elif kind == "even":
            wa += [units_of(ev_columns(a["ev_w_in_2"][0])), units_of(ev_rows(a["ev_w_out_2"][0]))]
        elif kind == "odd":
            wa += [units_of(od_columns(a["od_w_in_2"][0])), units_of(a["od_w_out_2"][0])]
        elif kind == "ffn1":
            wa.append(up_units(a["w_up"][l][:, :ff], a["w_up"][l][:, ff:]))
            wb.append(down_units(a["w_down"][l]))
        else:
            i, j = l // 2, l % 2
            wa.append(up_units(pad_to(a["ffn_w_gate_2"][i, j], ff, 1), pad_to(a["ffn_w_up_2"][i, j], ff, 1)))
            wb.append(down_units(pad_to(a["ffn_w_down_2"][i, j], ff, 0)))

    def both_heads(g):
        return np.concatenate([g, g])[:, None]

    def both_halves(g):
        return both_heads(pad_to(g, 64, 0))

    prm = np.concatenate(
        [per_chunk(a["attn_norm"]), per_chunk(a["ffn_norm"]), per_chunk(a["norm_g_2"]), per_chunk(a["conv_w"]),
         per_chunk(a["conv_b"])]
        + [both_heads(a["a_q_norm"][l]) for l in range(2)] + [both_heads(a["a_k_norm"][l]) for l in range(2)]
        + [both_halves(a["b_q_norm"][l]) for l in range(2)] + [both_halves(a["b_k_norm"][l]) for l in range(2)]
        + [per_chunk(a["c_lb_logits"]), a["ev_conv_w_2"][0].reshape(31, 4, P).transpose(2, 1, 0).reshape(P, 124),
           per_chunk(a["ev_conv_b_2"]), per_chunk(a["ev_ln_g_2"]), per_chunk(a["ev_ln_b_2"]),
           both_heads(a["ev_q_norm_g_2"][0]), both_heads(a["ev_k_norm_g_2"][0]), both_heads(a["od_q_norm_g_2"][0]),
           both_heads(a["od_k_norm_g_2"][0]), per_chunk(a["od_pool_scale_2"])], 1)
    row = np.concatenate([a["b_lambda"].ravel(), a["b_sub_norm"].ravel(), a["c_out_norm"].ravel(), a["ev_sinks_2"].ravel()])
    const, bias, mask = shape_constants()
    ins = {
        "x": a["x"][0].T.reshape(DC, P, SEQ).transpose(1, 0, 2).reshape(P, DC * SEQ),
        "wa": np.concatenate(wa, 0), "wb": np.concatenate(wb, 0), "prm": prm, "row": row[None, :],
        "const": const, "bias": bias, "mask": mask, "pool_w": a["od_pool_w_2"][0].transpose(1, 0, 2),
    }
    ins = {f"in_{k}": np.ascontiguousarray(v) for k, v in ins.items()}
    nc = _bacc.Bacc("TRN2", target_bir_lowering=False, num_devices=1)
    args = [nc.dram_tensor(k, v.shape, _mybir.dt.from_np(v.dtype), kind="ExternalInput").ap() for k, v in ins.items()]
    args.append(nc.dram_tensor("out_x", (P, DC * SEQ), _mybir.dt.float32, kind="ExternalOutput").ap())
    build_program(nc, *args)
    r = _run(nc, [ins], core_ids=[0])
    y = r.results[0]["out_x"]
    return y.reshape(P, DC, SEQ).transpose(1, 0, 2).reshape(D, SEQ).T[None]
```
